# Optimizing a Trainium2 kernel written in Bass

```python
import math
import jax
import jax.numpy as jnp
from jax import lax
import numpy as np
import jax, jax.numpy as jnp

D_MODEL = 1024
BATCH = 1
SEQ = 512
DEPTH = 2

N_MIXERS = 2
POOL_WINDOWS = (2, 4, 8, 16)
N_POOL_GROUPS = len(POOL_WINDOWS)
POOL_GROUP_DIM = D_MODEL // N_POOL_GROUPS
HEAD_DIM = 64
N_HEADS = D_MODEL // HEAD_DIM
DIL_CONFIGS = ((128, 1), (512, 4), (2048, 16))
N_DIL_GROUPS = len(DIL_CONFIGS)
ATTN_WIDTH = N_HEADS * HEAD_DIM
QKV_WIDTH = N_DIL_GROUPS * 3 * ATTN_WIDTH
D_FF = 2816
MACARON_WEIGHT = 0.5
ALPHA = (2.0 * DEPTH) ** 0.25
BETA = (8.0 * DEPTH) ** -0.25
LN_EPS = 1e-5
MASK_VALUE = -1e30


def _alibi_slopes():
    n = N_DIL_GROUPS * N_HEADS
    s = 2.0 ** (-8.0 * np.arange(1, n + 1) / n)
    return s.reshape(N_DIL_GROUPS, N_HEADS).astype(np.float32)

def _layer_norm(x, g, b):
    x32 = x.astype(jnp.float32)
    mu = jnp.mean(x32, axis=-1, keepdims=True)
    var = jnp.mean(jnp.square(x32 - mu), axis=-1, keepdims=True)
    y = (x32 - mu) * lax.rsqrt(var + LN_EPS)
    return (y * g.astype(jnp.float32) + b.astype(jnp.float32)).astype(x.dtype)

def _swiglu(x, w_gate, w_up, w_down):
    return (jax.nn.silu(x @ w_gate) * (x @ w_up)) @ w_down

def _pool_mixer(x, w_in, w_group, scale, w_out):
    B, S, _ = x.shape
    u = (x @ w_in).reshape(B, S, N_POOL_GROUPS, POOL_GROUP_DIM).astype(jnp.float32)
    csum = jnp.concatenate([jnp.zeros_like(u[:, :1]), jnp.cumsum(u, axis=1)], axis=1)
    half = jnp.asarray([w // 2 for w in POOL_WINDOWS], dtype=jnp.int32)
    t = jnp.arange(S, dtype=jnp.int32)[:, None]
    lo = jnp.clip(t - half[None, :], 0, S)
    hi = jnp.clip(t + half[None, :], 0, S)
    gidx = jnp.arange(N_POOL_GROUPS)[None, :]
    win_sum = csum[:, hi, gidx] - csum[:, lo, gidx]
    mean = win_sum / (hi - lo).astype(jnp.float32)[None, :, :, None]
    mixed = (mean - u).astype(x.dtype)
    y = jnp.einsum('bsgc,gce->bsge', mixed, w_group).reshape(B, S, D_MODEL) * scale
    return y @ w_out

def _dilated_group(q, k, v, window, dilation, slopes):
    B, S, H, E = q.shape
    d = dilation
    L = S // d
    R = window // (2 * d)
    W = R
    nb = -(-L // W)
    Lp = nb * W

    def to_sub(a):
        return a.reshape(B, L, d, H, E).transpose(0, 2, 3, 1, 4)

    qs = jnp.pad(to_sub(q), ((0, 0),) * 3 + ((0, Lp - L), (0, 0))).reshape(B, d, H, nb, W, E)

    def windows(a):
        ap = jnp.pad(to_sub(a), ((0, 0),) * 3 + ((W, W + Lp - L), (0, 0)))
        ap = ap.reshape(B, d, H, nb + 2, W, E)
        return jnp.concatenate([ap[:, :, :, :-2], ap[:, :, :, 1:-1], ap[:, :, :, 2:]], axis=4)

    kw = windows(k)
    vw = windows(v)
    a_idx = jnp.arange(W)
    c_idx = jnp.arange(3 * W)
    n_idx = jnp.arange(nb)
    rel = c_idx[None, :] - W - a_idx[:, None]
    j = (n_idx[:, None, None] - 1) * W + c_idx[None, None, :]
    valid = (jnp.abs(rel)[None] <= R) & (j >= 0) & (j < L)
    dist = (d * jnp.abs(rel)).astype(jnp.float32)
    bias = -slopes[:, None, None] * dist[None]
    scores = jnp.einsum('bdhnqe,bdhnke->bdhnqk', qs.astype(jnp.float32),
                        kw.astype(jnp.float32)) * (E ** -0.5) + bias[:, None]
    scores = jnp.where(valid, scores, MASK_VALUE)
    lse = jax.nn.logsumexp(scores, axis=-1)
    p = jnp.exp(scores - lse[..., None])
    o = jnp.einsum('bdhnqk,bdhnke->bdhnqe', p, vw.astype(jnp.float32))
    o = o.reshape(B, d, H, Lp, E)[:, :, :, :L].transpose(0, 3, 1, 2, 4).reshape(B, S, H, E)
    lse = lse.reshape(B, d, H, Lp)[..., :L].transpose(0, 3, 1, 2).reshape(B, S, H)
    return o, lse

def _dilated_attention_mixer(x, w_qkv, w_out):
    B, S, _ = x.shape
    qkv = (x @ w_qkv).reshape(B, S, N_DIL_GROUPS, 3, N_HEADS, HEAD_DIM)
    slopes = jnp.asarray(_alibi_slopes())
    outs, lses = [], []
    for g, (window, dil) in enumerate(DIL_CONFIGS):
        o, l = _dilated_group(qkv[:, :, g, 0], qkv[:, :, g, 1], qkv[:, :, g, 2],
                              window, dil, slopes[g])
        outs.append(o)
        lses.append(l)
    wts = jax.nn.softmax(jnp.stack(lses), axis=0)
    o = jnp.sum(wts[..., None] * jnp.stack(outs), axis=0)
    return o.reshape(B, S, ATTN_WIDTH).astype(x.dtype) @ w_out

def first_inputs(seed: int = 0) -> dict:
    key = jax.random.key(seed)
    ks = jax.random.split(key, 16)
    n_pool = (DEPTH + 1) // 2
    n_attn = DEPTH // 2
    f32 = jnp.float32

    def nrm(k, shape, scale):
        return jax.random.normal(k, shape, f32) * scale

    return {
        "x": jax.random.normal(ks[0], (BATCH, SEQ, D_MODEL), f32),
        "ffn1_w_gate": nrm(ks[1], (DEPTH, D_MODEL, D_FF), D_MODEL ** -0.5),
        "ffn1_w_up": nrm(ks[2], (DEPTH, D_MODEL, D_FF), D_MODEL ** -0.5),
        "ffn1_w_down": nrm(ks[3], (DEPTH, D_FF, D_MODEL), BETA * D_FF ** -0.5),
        "ffn2_w_gate": nrm(ks[4], (DEPTH, D_MODEL, D_FF), D_MODEL ** -0.5),
        "ffn2_w_up": nrm(ks[5], (DEPTH, D_MODEL, D_FF), D_MODEL ** -0.5),
        "ffn2_w_down": nrm(ks[6], (DEPTH, D_FF, D_MODEL), BETA * D_FF ** -0.5),
        "ln_gain": 1.0 + nrm(ks[7], (DEPTH, 3, D_MODEL), 0.02),
        "ln_bias": nrm(ks[8], (DEPTH, 3, D_MODEL), 0.02),
        "pool_w_in": nrm(ks[9], (n_pool, D_MODEL, D_MODEL), D_MODEL ** -0.5),
        "pool_w_group": nrm(ks[10], (n_pool, N_POOL_GROUPS, POOL_GROUP_DIM, POOL_GROUP_DIM),
                            POOL_GROUP_DIM ** -0.5),
        "pool_scale": 1.0 + nrm(ks[11], (n_pool, D_MODEL), 0.1),
        "pool_w_out": nrm(ks[12], (n_pool, D_MODEL, D_MODEL), BETA * D_MODEL ** -0.5),
        "attn_w_qkv": nrm(ks[13], (n_attn, D_MODEL, QKV_WIDTH), D_MODEL ** -0.5),
        "attn_w_out": nrm(ks[14], (n_attn, ATTN_WIDTH, D_MODEL), BETA * ATTN_WIDTH ** -0.5),
    }

def first_block(x, ffn1_w_gate, ffn1_w_up, ffn1_w_down, ffn2_w_gate, ffn2_w_up, ffn2_w_down,
              ln_gain, ln_bias, pool_w_in, pool_w_group, pool_scale, pool_w_out,
              attn_w_qkv, attn_w_out):
    for i in range(DEPTH):
        h = _swiglu(x, ffn1_w_gate[i], ffn1_w_up[i], ffn1_w_down[i])
        x = _layer_norm(ALPHA * x + MACARON_WEIGHT * h, ln_gain[i, 0], ln_bias[i, 0])
        if i % N_MIXERS == 0:
            p = i // N_MIXERS
            m = _pool_mixer(x, pool_w_in[p], pool_w_group[p], pool_scale[p], pool_w_out[p])
        else:
            a = i // N_MIXERS
            m = _dilated_attention_mixer(x, attn_w_qkv[a], attn_w_out[a])
        x = _layer_norm(ALPHA * x + m, ln_gain[i, 1], ln_bias[i, 1])
        h = _swiglu(x, ffn2_w_gate[i], ffn2_w_up[i], ffn2_w_down[i])
        x = _layer_norm(ALPHA * x + MACARON_WEIGHT * h, ln_gain[i, 2], ln_bias[i, 2])
    return x


RET_HEADS = 4
RET_DK = 64
RET_DV = 128
RET_CHUNK = 128
RET_THETA = 10000.0
DSA_HEADS = 8
DSA_KV_HEADS = 2
DSA_DH = 64
DSA_ROT = DSA_DH // 4
ROPE_THETA = 500000.0
IDX_HEADS = 4
IDX_DH = 64
IDX_ROT = IDX_DH // 4
TOPK_MAX = 256
Q_BLOCK = 128
GLA_HEADS = 4
GLA_DK = 64
GLA_DV = 128
GLA_RANK = 16
GLA_TAU = 16.0
GLA_CHUNK = 64

N_BRANCH = 3
RMS_EPS = 1e-6
RET_W = RET_HEADS * RET_DV
DSA_W = DSA_HEADS * DSA_DH
GLA_W = GLA_HEADS * GLA_DV

IN_SPLITS = (
    ("ret_q", RET_HEADS * RET_DK), ("ret_k", RET_HEADS * RET_DK),
    ("ret_v", RET_W), ("ret_g", RET_W),
    ("dsa_q", DSA_W), ("dsa_k", DSA_KV_HEADS * DSA_DH), ("dsa_v", DSA_KV_HEADS * DSA_DH),
    ("dsa_g", DSA_W),
    ("idx_q", IDX_HEADS * IDX_DH), ("idx_k", IDX_DH), ("idx_w", IDX_HEADS),
    ("gla_q", GLA_HEADS * GLA_DK), ("gla_k", GLA_HEADS * GLA_DK),
    ("gla_v", GLA_W), ("gla_g", GLA_W), ("gla_a", GLA_RANK),
    ("merge", N_BRANCH * D_MODEL),
)
IN_WIDTH = sum(w for _, w in IN_SPLITS)


def rms_norm(x, gain=None):
    xf = x.astype(jnp.float32)
    y = xf * lax.rsqrt(jnp.mean(xf * xf, axis=-1, keepdims=True) + RMS_EPS)
    if gain is not None:
        y = y * gain.astype(jnp.float32)
    return y.astype(x.dtype)

def split_proj(p):
    bounds = np.cumsum([w for _, w in IN_SPLITS])[:-1].tolist()
    parts = jnp.split(p, bounds, axis=-1)
    return {name: t for (name, _), t in zip(IN_SPLITS, parts)}

def rope(x, pos, rot_dim, theta):
    half = rot_dim // 2
    freqs = theta ** (-jnp.arange(half, dtype=jnp.float32) * 2.0 / rot_dim)
    ang = pos.astype(jnp.float32)[..., None] * freqs
    cos = jnp.cos(ang)[:, :, None, :]
    sin = jnp.sin(ang)[:, :, None, :]
    xf = x.astype(jnp.float32)
    x1 = xf[..., :half]
    x2 = xf[..., half:rot_dim]
    out = jnp.concatenate([x1 * cos - x2 * sin, x2 * cos + x1 * sin, xf[..., rot_dim:]], axis=-1)
    return out.astype(x.dtype)

def retention(q, k, v, pos):
    dt = v.dtype
    B, S, H, dk = q.shape
    dv = v.shape[-1]
    C = RET_CHUNK
    n = S // C
    q = rope(q, pos, dk, RET_THETA).astype(jnp.float32) * (dk ** -0.5)
    k = rope(k, pos, dk, RET_THETA).astype(jnp.float32)
    v = v.astype(jnp.float32)
    log_g = jnp.log1p(-jnp.exp2(-5.0 - jnp.arange(H, dtype=jnp.float32)))
    idx = jnp.arange(C, dtype=jnp.float32)
    rel = idx[:, None] - idx[None, :]
    decay = jnp.where(rel >= 0, jnp.exp(log_g[:, None, None] * jnp.maximum(rel, 0.0)), 0.0)
    qc = q.reshape(B, n, C, H, dk)
    kc = k.reshape(B, n, C, H, dk)
    vc = v.reshape(B, n, C, H, dv)
    scores = jnp.einsum('bnihd,bnjhd->bnhij', qc, kc) * decay
    o_intra = jnp.einsum('bnhij,bnjhe->bnihe', scores, vc)
    to_end = jnp.exp((C - 1 - idx)[:, None] * log_g[None, :])
    kv = jnp.einsum('bnjhd,bnjhe->bnhde', kc * to_end[None, None, :, :, None], vc)
    chunk_decay = jnp.exp(C * log_g)[None, :, None, None]

    def step(state, kv_n):
        return chunk_decay * state + kv_n, state

    _, prev = lax.scan(step, jnp.zeros((B, H, dk, dv), jnp.float32), jnp.moveaxis(kv, 1, 0))
    prev = jnp.moveaxis(prev, 0, 1)
    q_dec = qc * jnp.exp((idx + 1.0)[:, None] * log_g[None, :])[None, None, :, :, None]
    o_cross = jnp.einsum('bnihd,bnhde->bnihe', q_dec, prev)
    return (o_intra + o_cross).reshape(B, S, H, dv).astype(dt)

def gla(q, k, v, log_a):
    dt = v.dtype
    B, S, H, dk = q.shape
    dv = v.shape[-1]
    C = GLA_CHUNK
    n = S // C
    q = q.astype(jnp.float32) * (dk ** -0.5)
    k = k.astype(jnp.float32)
    v = v.astype(jnp.float32)
    log_a = log_a.astype(jnp.float32)
    causal = jnp.tril(jnp.ones((C, C), bool))

    def to_chunks(t):
        return jnp.moveaxis(t.reshape(B, n, C, H, t.shape[-1]), 1, 0)

    def step(state, inp):
        qn, kn, vn, an = inp
        bcum = jnp.cumsum(an, axis=1)
        diff = bcum[:, :, None] - bcum[:, None, :]
        w = jnp.exp(jnp.where(causal[None, :, :, None, None], diff, -jnp.inf))
        attn = jnp.einsum('bihd,bjhd,bijhd->bhij', qn, kn, w)
        o = (jnp.einsum('bhij,bjhe->bihe', attn, vn)
             + jnp.einsum('bihd,bhde->bihe', qn * jnp.exp(bcum), state))
        b_last = bcum[:, -1]
        new = (jnp.exp(b_last)[..., None] * state
               + jnp.einsum('bjhd,bjhe->bhde', kn * jnp.exp(b_last[:, None] - bcum), vn))
        return new, o

    _, o = lax.scan(step, jnp.zeros((B, H, dk, dv), jnp.float32),
                    (to_chunks(q), to_chunks(k), to_chunks(v), to_chunks(log_a)))
    return jnp.moveaxis(o, 0, 1).reshape(B, S, H, dv).astype(dt)

def dsa_attention(q, k, v, q_idx, k_idx, w_idx, pos):
    B, S, H, dh = q.shape
    KV = k.shape[2]
    G = H // KV
    topk = min(TOPK_MAX, S // 4)
    QB = Q_BLOCK
    nb = S // QB
    q = rope(q, pos, DSA_ROT, ROPE_THETA)
    k = rope(k, pos, DSA_ROT, ROPE_THETA)
    q_idx = rope(q_idx, pos, IDX_ROT, ROPE_THETA)
    k_idx_f = rope(k_idx[:, :, None], pos, IDX_ROT, ROPE_THETA)[:, :, 0].astype(jnp.float32)
    w_f = w_idx.astype(jnp.float32) * (IDX_HEADS ** -0.5)
    key_pos = jnp.arange(S)

    def blockify(t):
        return jnp.moveaxis(t.reshape(B, nb, QB, *t.shape[2:]), 1, 0)

    def one_block(inp):
        qb, qib, wb, tb = inp
        s = jnp.einsum('bqhd,bsd->bqhs', qib.astype(jnp.float32), k_idx_f) * (IDX_DH ** -0.5)
        score = jnp.einsum('bqh,bqhs->bqs', wb, jax.nn.relu(s))
        visible = key_pos[None, :] <= tb[:, None]
        score = jnp.where(visible[None], score, -jnp.inf)
        _, sel = lax.top_k(score, topk)
        valid = sel <= tb[None, :, None]
        ks = jax.vmap(lambda kk, ii: kk[ii])(k, sel)
        vs = jax.vmap(lambda vv, ii: vv[ii])(v, sel)
        qg = qb.reshape(B, QB, KV, G, dh)
        logits = jnp.einsum('bqngd,bqknd->bqngk', qg, ks).astype(jnp.float32) * (dh ** -0.5)
        logits = jnp.where(valid[:, :, None, None, :], logits, -jnp.inf)
        p = jax.nn.softmax(logits, axis=-1).astype(vs.dtype)
        o = jnp.einsum('bqngk,bqknd->bqngd', p, vs)
        return o.reshape(B, QB, H * dh)

    t_blocks = jnp.arange(S).reshape(nb, QB)
    out = lax.map(one_block, (blockify(q), blockify(q_idx), blockify(w_f), t_blocks))
    return jnp.moveaxis(out, 0, 1).reshape(B, S, H * dh)

def second_inputs(seed: int = 0) -> dict:
    key = jax.random.key(seed)
    ks = jax.random.split(key, 16)
    D = D_MODEL
    nrm = jax.random.normal
    x = nrm(ks[0], (BATCH, SEQ, D), jnp.float32)
    c = nrm(ks[1], (BATCH, D), jnp.float32)
    positions = (jnp.arange(SEQ, dtype=jnp.int32)[None, :]
                 + jax.random.randint(ks[2], (BATCH, 1), 0, 4096, dtype=jnp.int32))
    ada_w = nrm(ks[3], (DEPTH, D, 3 * D), jnp.float32) * (0.1 * D ** -0.5)
    ada_b = nrm(ks[4], (DEPTH, 3 * D), jnp.float32) * 0.02
    pre_norm = 1.0 + 0.05 * nrm(ks[5], (DEPTH, D), jnp.float32)
    post_norm = 1.0 + 0.05 * nrm(ks[6], (DEPTH, D), jnp.float32)
    w_in = nrm(ks[7], (DEPTH, D, IN_WIDTH), jnp.float32) * (D ** -0.5)
    gla_w_lr = nrm(ks[8], (DEPTH, GLA_RANK, GLA_HEADS * GLA_DK), jnp.float32) * (GLA_RANK ** -0.5)
    gla_b_lr = 0.1 * nrm(ks[9], (DEPTH, GLA_HEADS * GLA_DK), jnp.float32)
    w_br_ret = nrm(ks[10], (DEPTH, RET_W, D), jnp.float32) * (RET_W ** -0.5)
    w_br_dsa = nrm(ks[11], (DEPTH, DSA_W, D), jnp.float32) * (DSA_W ** -0.5)
    w_br_gla = nrm(ks[12], (DEPTH, GLA_W, D), jnp.float32) * (GLA_W ** -0.5)
    w_out = nrm(ks[13], (DEPTH, D, D), jnp.float32) * (D ** -0.5)
    return {"x": x, "c": c, "positions": positions, "ada_w": ada_w, "ada_b": ada_b,
            "pre_norm": pre_norm, "post_norm": post_norm, "w_in": w_in,
            "gla_w_lr": gla_w_lr, "gla_b_lr": gla_b_lr, "w_br_ret": w_br_ret,
            "w_br_dsa": w_br_dsa, "w_br_gla": w_br_gla, "w_out": w_out}

def second_block(x, c, positions, ada_w, ada_b, pre_norm, post_norm, w_in, gla_w_lr, gla_b_lr,
              w_br_ret, w_br_dsa, w_br_gla, w_out):
    B, S, D = x.shape
    c_act = jax.nn.silu(c)
    for l in range(DEPTH):
        mod = c_act @ ada_w[l] + ada_b[l]
        shift, scale, gate = jnp.split(mod, 3, axis=-1)
        h = rms_norm(x, pre_norm[l]) * (1.0 + scale[:, None]) + shift[:, None]
        p = split_proj(h @ w_in[l])
        ret = retention(p["ret_q"].reshape(B, S, RET_HEADS, RET_DK),
                        p["ret_k"].reshape(B, S, RET_HEADS, RET_DK),
                        p["ret_v"].reshape(B, S, RET_HEADS, RET_DV), positions)
        ret = rms_norm(ret).reshape(B, S, RET_W) * jax.nn.silu(p["ret_g"])
        dsa = dsa_attention(p["dsa_q"].reshape(B, S, DSA_HEADS, DSA_DH),
                            p["dsa_k"].reshape(B, S, DSA_KV_HEADS, DSA_DH),
                            p["dsa_v"].reshape(B, S, DSA_KV_HEADS, DSA_DH),
                            p["idx_q"].reshape(B, S, IDX_HEADS, IDX_DH),
                            p["idx_k"], p["idx_w"], positions)
        dsa = dsa * jax.nn.silu(p["dsa_g"])
        log_a = jax.nn.log_sigmoid((p["gla_a"] @ gla_w_lr[l] + gla_b_lr[l]).astype(jnp.float32)) / GLA_TAU
        gl = gla(p["gla_q"].reshape(B, S, GLA_HEADS, GLA_DK),
                 p["gla_k"].reshape(B, S, GLA_HEADS, GLA_DK),
                 p["gla_v"].reshape(B, S, GLA_HEADS, GLA_DV),
                 log_a.reshape(B, S, GLA_HEADS, GLA_DK))
        gl = rms_norm(gl).reshape(B, S, GLA_W) * jax.nn.silu(p["gla_g"])
        g = jax.nn.sigmoid(p["merge"]).reshape(B, S, N_BRANCH, D)
        y = (g[:, :, 0] * (ret @ w_br_ret[l])
             + g[:, :, 1] * (dsa @ w_br_dsa[l])
             + g[:, :, 2] * (gl @ w_br_gla[l]))
        y = y @ w_out[l]
        x = x + gate[:, None] * rms_norm(y, post_norm[l])
    return x


def setup_inputs(seed=0):
    out = dict(first_inputs(seed))
    for name, value in second_inputs(seed + 1).items():
        if name != "x":
            out[name + "_2"] = value
    return out


def reference(
    x, ffn1_w_gate, ffn1_w_up, ffn1_w_down, ffn2_w_gate, ffn2_w_up, ffn2_w_down, ln_gain,
    ln_bias, pool_w_in, pool_w_group, pool_scale, pool_w_out, attn_w_qkv, attn_w_out, c_2,
    positions_2, ada_w_2, ada_b_2, pre_norm_2, post_norm_2, w_in_2, gla_w_lr_2, gla_b_lr_2,
    w_br_ret_2, w_br_dsa_2, w_br_gla_2, w_out_2,
):
    x = first_block(
        x, ffn1_w_gate, ffn1_w_up, ffn1_w_down, ffn2_w_gate, ffn2_w_up, ffn2_w_down, ln_gain,
        ln_bias, pool_w_in, pool_w_group, pool_scale, pool_w_out, attn_w_qkv, attn_w_out,
    )
    return second_block(
        x, c_2, positions_2, ada_w_2, ada_b_2, pre_norm_2, post_norm_2, w_in_2, gla_w_lr_2,
        gla_b_lr_2, w_br_ret_2, w_br_dsa_2, w_br_gla_2, w_out_2,
    )


_drawn_inputs = setup_inputs


def setup_inputs(seed=0):
    import zlib

    import numpy as np

    out = dict(_drawn_inputs(seed))
    spreads = {}
    factors = {'pre_norm_2': 5.792,
     'post_norm_2': 8.0,
     'gla_w_lr_2': 8.0,
     'gla_b_lr_2': 49.888,
     'w_br_dsa_2': 4.236}
    for name, (base, spread) in spreads.items():
        noise = np.random.default_rng([zlib.crc32(name.encode()), seed]).standard_normal(out[name].shape)
        drawn = base * np.exp(spread * noise) if base else spread * noise
        out[name] = jnp.asarray(drawn.astype(out[name].dtype))
    for name, factor in factors.items():
        out[name] = (out[name] * factor).astype(out[name].dtype)
    return out
```

```python
from contextlib import ExitStack, contextmanager

import numpy as np

import concourse.bass as bass
from concourse import mybir
from concourse.alu_op_type import AluOpType as ALU

ACT = mybir.ActivationFunctionType
AX = mybir.AxisListType
F32 = mybir.dt.float32
F32R = mybir.dt.float32r
I32 = mybir.dt.int32
U8 = mybir.dt.uint8

P = 128
T = 512
TT = T // P
D = 1024
KT = D // P
F = 2816
FT = F // P
DOWN_PARTS = (8, 7, 7)
DEPTH = 2
ADA_GROUP = DEPTH * 3 * D // (FT // 2 + 1)
ALPHA = (2.0 * DEPTH) ** 0.25
LN_EPS = 1e-5
RMS_EPS = 1e-6
GROUPS = 4
PAD = 8
HEADS = 16
E = 64
QUADS = 4
BIG = 1e30
TAKEN = -3e38
TOPK = 128
ROUND = 12582912.0
TWO_PI_A = 6.28125
TWO_PI_B = float(np.float32(np.round((2 * np.pi - 6.28125) * 2**22) / 2**22))
TWO_PI_C = float(2 * np.pi - TWO_PI_A - TWO_PI_B)
PI_SAFE = 3.1415925

RET_Q, RET_K, RET_V, RET_G = 0, 256, 512, 1024
DSA_Q, DSA_KV, DSA_G = 1536, 2048, 2304
IDX_Q, IDX_K = 2816, 3072
GLA_Q, GLA_K, GLA_V, GLA_G, GLA_A = 3140, 3396, 3652, 4164, 4676
MERGE = 4692


def constants():
    f32 = np.float32
    p = np.arange(P)
    c = {}
    c["identity"] = np.eye(P, dtype=f32)
    t = np.arange(T)
    inv = [1.0 / (np.minimum(t + h, T) - np.maximum(t - h, 0)).astype(f32) for h in (1, 2, 4, 8)]
    c["inv_count"] = np.concatenate(inv).astype(f32).reshape(1, GROUPS * T)
    r = np.arange(4)
    q_t = 4 * p[None, :, None, None] + r[:, None, None, None]
    k_t = 4 * p[None, None, None, :] + r[None, None, :, None]
    d0 = np.abs(q_t - k_t).astype(f32)
    c["dist0"] = np.where(d0 <= 64, d0, f32(BIG)).reshape(4, P, T).transpose(1, 0, 2).reshape(P, 4 * T).astype(f32)
    pd = np.abs(p[:, None] - p[None, :])
    d1 = np.where(pd <= 64, 4.0 * pd, BIG).astype(f32)
    d2 = np.where(pd % 4 == 0, 4.0 * pd, BIG).astype(f32)
    c["dist12"] = np.concatenate([d1, d2], axis=1)
    n = 3 * HEADS
    slopes = (2.0 ** (-8.0 * np.arange(1, n + 1) / n)).astype(f32).reshape(3, HEADS)
    c["slopes"] = (slopes.reshape(3, QUADS, 4).transpose(1, 0, 2)).reshape(1, n).astype(f32)
    for name, rot, theta in (("ret", 64, 10000.0), ("dsa", 16, 500000.0)):
        half = rot // 2
        freq = np.zeros(64, f32)
        base = (theta ** (-np.arange(half) * 2.0 / rot)).astype(f32)
        freq[:half] = base
        freq[half:rot] = base
        swap = np.zeros((64, 64), f32)
        for i in range(half):
            swap[i, i + half] = -1.0
            swap[i + half, i] = 1.0
        c["freq_" + name] = np.tile(freq, 2).reshape(P, 1)
        c["swap_" + name] = np.kron(np.eye(2, dtype=f32), swap).T.copy()
    log_g = np.log1p(-np.exp2(-5.0 - np.arange(4, dtype=f32))).astype(f32)
    rel = (np.arange(T)[None, :] - p[:, None]).astype(f32)
    decay = [np.where(rel >= 0, np.exp(lg * np.maximum(rel, 0)), 0.0) for lg in log_g]
    c["decay"] = np.concatenate(decay, axis=1).astype(f32)
    c["causal"] = np.where(p[None, :] > p[:, None], f32(-BIG), f32(0)).astype(f32)
    masks = []
    for l in range(7):
        b = p >> l
        masks.append((b[None, :] % 2 == 1) & (b[:, None] == b[None, :] - 1))
    masks.append(p[:, None] == p[None, :])
    c["level_masks"] = np.concatenate(masks, axis=1).astype(np.int32)
    return c


CONSTANTS = constants()


class Signal:

    def __init__(self, sem):
        self.sem, self.made, self.rolled = sem, 0, None

    def now(self):
        return self.made if self.rolled is None else self.rolled + self.made

    def up(self, ins):
        ins.then_inc(self.sem, 1)
        self.made += 1
        return self.now()


@contextmanager
def rolled(eng, count, raised):
    with eng.Fori(0, count) as i:
        before = {}
        for s, per in raised.items():
            before[s] = (s.made, s.rolled)
            s.rolled = i * per if s.rolled is None else s.rolled + i * per
        yield i
    for s, per in raised.items():
        made, outer = before[s]
        assert s.made == made + per, (s.sem, s.made - made, per)
        s.made, s.rolled = made + per * count, outer


FFN = dict(gate_act=FT, hid=FT, hid_hi=FT, hid_lo=FT, z_ready=KT)
PAIRS = KT // 2
NORM = dict(zsum_ready=1, mean_ready=1, dev_ready=KT, sq_ready=KT, sq_pair=PAIRS, var_part=PAIRS, std_ready=1, t_ready=KT,
            x_ready=KT, xh_ready=KT, acts=KT)
POOLED = dict(u_ready=KT, mixed=KT, mixed_hi=KT, mixed_lo=KT, y_full=KT, y_hi=KT, y_lo=KT, z_ready=KT)
UNIT_SIGNALS = ("scored", "nbias", "probs", "t_done", "pt_copied", "pv_done", "normed")
ATTN_UNITS = HEADS * 4
ATTN = dict({k: ATTN_UNITS for k in UNIT_SIGNALS}, sc_ready=3 * ATTN_UNITS, lin_ev=18 * QUADS,
            qk_low=4 * QUADS, o_hi=2 * QUADS, o_lo=2 * QUADS, z_ready=KT)


MIXER_ORDER = ("idx_q", "idx_k", "dsa_q0", "dsa_q1", "dsa_kv", "dsa_g0", "dsa_g1", "mix_dsa",
               "ret_q", "ret_k", "ret_v0", "ret_v1", "ret_g0", "ret_g1", "mix_ret",
               "gla_q", "gla_k", "gla_v0", "gla_v1", "gla_g0", "gla_g1", "gla_a", "mix_gla", "out")
INDEX_UNITS = 3 * 4
DSA_UNITS = 4 * 8
ROPES = 3 + 5 + 4
EARLY_ROUNDS = 8
LEVELS = 9
MIXER = dict({k: DSA_UNITS for k in UNIT_SIGNALS}, sc_ready=DSA_UNITS,
             lin_ev=40 + 24 + 8, rot=ROPES, rope_done=ROPES, idx_mm=INDEX_UNITS, idx_relu=INDEX_UNITS,
             idx_acc=INDEX_UNITS, kd_ready=4, ikd_ready=1, br_full=12, br_hi=12, br_lo=12, mixed=24,
             ret_mm=16, st_ready=16, head_done=8, hsq=8, hvar=8, hstd=8, lr_mm=2, la_parts=2, la_ready=2,
             ex_ready=2 * LEVELS * 2, qk_ready=2 * LEVELS * 2, lvl_mm=2 * 2 * 10, lvl_cp=2 * 2 * 8,
             sq_ready=2 * KT, sq_pair=2 * PAIRS, var_part=2 * PAIRS, std_ready=2, t_ready=2 * KT, h_ready=KT, xh_ready=2 * KT, acts=2 * KT,
             la_next=2 * (LEVELS - 1), so_cp=8, sd_zero=2, x_out=KT)


class Stage:
    def __init__(self, kind, index, per, base, chunk0):
        self.kind, self.index, self.per, self.base, self.chunk0 = kind, index, per, base, chunk0
        self.index_in_kind = 0

    def at(self, name, n):
        return self.base.get(name, 0) + n


def add(*parts):
    out = {}
    for part in parts:
        for k, v in part.items():
            out[k] = out.get(k, 0) + v
    return out


PRIMED = dict(acc=4, w_lo=2, gate_act=2, hid=2, hid_lo=2, z_ready=4)
SIGNALS = ("acc w_hi w_lo gate_act hid hid_hi hid_lo z_ready zsum_ready mean_ready dev_ready sq_ready sq_pair "
           "var_part std_ready t_ready x_ready xh_ready acts dve_step act_step "
           "u_ready y_mm mixed mixed_hi mixed_lo y_full y_hi y_lo "
           "scored qk_low sc_ready nbias probs t_done pt_copied pv_done normed lin_ev o_hi o_lo "
           "rot rope_done angles waves idx_mm idx_relu idx_acc kd_ready ikd_ready br_full br_hi br_lo "
           "ret_mm st_ready head_done hsq hvar hstd lr_mm la_parts la_ready ex_ready qk_ready lvl_mm lvl_cp "
           "h_ready x_out ada_mul ada_mm ada_out mod_ready la_next so_cp sd_zero").split()


class Kernel:

    def __init__(self, nc, dram, stages, ctx):
        self.nc, self.dram, self.ctx = nc, dram, ctx
        self.plan(stages)
        sb = self.sb
        self.x = sb("x", [P, KT, T])
        self.xh = sb("xh", [P, KT, T], F32R)
        with ExitStack() as own:
            self.squares = sb("squares", [P, KT, T], ctx=own)
        self.xl = sb("xl", [P, KT, T], F32R)
        self.w_raw = sb("w_raw", [P, 2, 8 * 256])
        self.wh = sb("wh", [P, 2, 8 * 256], F32R)
        self.wl = sb("wl", [P, 2, 8 * 256], F32R)
        self.zero = sb("zero", [P, 1])
        self.ones = sb("ones", [P, P])
        self.eps = sb("eps", [P, 4])
        self.ln = sb("ln", [P, 2, 6, KT])
        self.identity = sb("identity", [P, P])
        self.pool_scale = sb("pool_scale", [P, KT])
        self.slopes = sb("slopes", [P, 3 * HEADS])
        self.norms = sb("norms", [P, 2, DEPTH, KT])
        self.ada_b = sb("ada_b", [P, DEPTH, 3 * KT])
        self.lr_b = sb("lr_b", [P, DEPTH, 2])
        self.c_act = sb("c_act", [P, KT])
        self.mod = sb("mod", [P, DEPTH, 3 * KT])
        self.sq = sb("sq", [P, 2, T])
        self.stats = sb("stats", [P, 2, T])
        self.zsum, self.std = self.stats[:, 0], self.stats[:, 1]
        self.ps = ctx.enter_context(nc.psum_tensor("ps", [P, 8, T], F32))
        sem = lambda n: ctx.enter_context(nc.semaphore(n))
        self.s = {n: Signal(sem(n)) for n in SIGNALS}
        for n, v in PRIMED.items():
            self.s[n].made = v
        self.landed = [sem("landed_even"), sem("landed_odd")]
        self.x_in = sem("x_in")
        self.consts_in = sem("consts_in")
        self.out_done = sem("out_done")
        self.setup = sem("setup")
        self.tables_in = sem("tables_in")
        self.lr_in = sem("lr_in")
        self.ada_in = [sem("ada_even"), sem("ada_odd")]
        self.allocate()

    def sb(self, name, shape, dt=F32, ctx=None):
        return (ctx or self.ctx).enter_context(self.nc.sbuf_tensor(name, shape, dt))

    def plan(self, stages):
        self.stages, self.segments, chunk = [], [], 0
        base = dict(PRIMED)
        for kind, index in stages:
            per, segs = self.describe(kind)(index)
            self.stages.append(Stage(kind, index, per, dict(base), chunk))
            self.stages[-1].index_in_kind = sum(o.kind == kind for o in self.stages) - 1
            for count, loads in segs:
                assert count == 1 or len(loads) % 2 == 0
                self.segments.append((chunk, count, loads))
                chunk += count * len(loads)
            for k, v in per.items():
                base[k] = base.get(k, 0) + v
        self.end = base
        self.chunks = chunk

    def describe(self, kind):
        return dict(start=self.stage_start, ffn=self.stage_ffn, pool=self.stage_pool, attn=self.stage_attn,
                    mixer=self.stage_mixer, end=self.stage_end)[kind]

    def allocate(self):
        kinds = {s.kind for s in self.stages}
        self.mixes = "mixer" in kinds
        for kind, make in (("ffn", self.memory_ffn), ("pool", self.memory_pool), ("attn", self.memory_attn),
                           ("mixer", self.memory_mixer)):
            if kind in kinds:
                with ExitStack() as own:
                    make(own)

    def chunk_source(self, load, i):
        w, k0, k, (first, per), width = load
        col = first + per * i if per else first
        return w.rearrange("(k p) n -> p k n", p=P)[:, k0:k0 + k, bass.ds(col, width)], k, width

    def each_chunk(self, eng, raised, body):
        for c0, count, loads in self.segments:
            if count == 1:
                for q, load in enumerate(loads):
                    body(c0 + q, (c0 + q) // 2, (c0 + q) % 2, load, 0)
            else:
                n = len(loads)
                with rolled(eng, count, {self.s[k]: n for k in raised}) as i:
                    for q, load in enumerate(loads):
                        body(c0 + q + i * n, (c0 + q) // 2 + i * (n // 2), (c0 + q) % 2, load, i)

    def sp_weights(self, sp):
        def load(c, turn, slot, spec, i):
            src, k, width = self.chunk_source(spec, i)
            sp.wait_ge(self.s["w_lo"].sem, c + 1)
            dst = self.w_raw[:, slot, 0:k * width].rearrange("p (k n) -> p k n", k=k)
            sp.dma_start(dst, src).then_inc(self.landed[slot], 16)
        self.each_chunk(sp, (), load)

    def pool_weights(self, pool):
        s = self.s
        pool.wait_ge(self.setup, 1)
        def split(c, turn, slot, spec, i):
            n = spec[2] * spec[4]
            raw, hi, lo = (b[:, slot, 0:n] for b in (self.w_raw, self.wh, self.wl))
            pool.wait_ge(self.landed[slot], turn * 16 + 16)
            pool.wait_ge(s["acc"].sem, 2 * c + 2)
            t = s["w_hi"].up(pool.tensor_tensor(hi, raw, self.zero[:, 0:1].to_broadcast([P, n]), ALU.subtract))
            pool.wait_ge(s["w_hi"].sem, t)
            s["w_lo"].up(pool.tensor_tensor(lo, raw, hi.bitcast(F32), ALU.subtract))
        self.each_chunk(pool, ("w_hi", "w_lo"), split)

    def acc(self, c, half):
        return PRIMED["acc"] + 2 * c + half + 1

    def wait_chunk(self, pe, c):
        pe.wait_ge(self.s["w_lo"].sem, PRIMED["w_lo"] + c + 1)

    def product(self, pe, slot, k, width, c0, out, xs, start=True, stop=True, before=None, count=True, t0=0):
        xh, xl = xs
        for t in range(k):
            if before:
                before(t)
            w = slice((t0 + t) * width + c0, (t0 + t) * width + c0 + P)
            for q, (a, b) in enumerate(((self.wh, xh), (self.wh, xl), (self.wl, xh))):
                mm = self.nc.tensor.matmul(out, a[:, slot, w], b(t), start=start and t == 0 and q == 0,
                                           stop=stop and t == k - 1 and q == 2)
        if count:
            self.s["acc"].up(mm)
        return mm

    def x_tile(self, pe, st, later=0):
        return lambda t: pe.wait_ge(self.s["acts"].sem, st.at("acts", t + 1 - KT + later))

    def x_parts(self):
        return (lambda t: self.xh[:, t, :]), (lambda t: self.xl[:, t, :])

    def stage_start(self, index):
        return dict(xh_ready=KT, acts=KT), []

    def consts(self):
        d = self.dram
        return [(self.ln[:], d["ln"].rearrange("p (a u k) -> p a u k", a=2, u=6)),
                (self.identity[:], d["const_identity"]),
                (self.pool_scale[:], d["pool_scale"]),
                (self.slopes[:], d["const_slopes"].to_broadcast([P, 3 * HEADS])),
                (self.norms[:, 0], d["pre_norm_2"].rearrange("p (l k) -> p l k", l=DEPTH)),
                (self.norms[:, 1], d["post_norm_2"].rearrange("p (l k) -> p l k", l=DEPTH)),
                (self.ada_b[:], d["ada_b_2"].rearrange("p (l n) -> p l n", l=DEPTH)),
                (self.lr_b[:], d["gla_b_lr_2"].rearrange("p (l n) -> p l n", l=DEPTH)),
                (self.c_act[:], d["c_2"])]

    def wait_consts(self, eng):
        eng.wait_ge(self.consts_in, 16 * len(self.consts()))

    def act_start(self, act, st):
        act.sem_inc(self.s["gate_act"].sem, PRIMED["gate_act"])
        act.dma_start(self.x[:], self.dram["x_t"].rearrange("(k p) t -> p k t", p=P)).then_inc(self.x_in, 16)
        for dst, src in self.consts():
            act.dma_start(dst, src).then_inc(self.consts_in, 16)
        act.wait_ge(self.setup, 6)
        act.wait_ge(self.x_in, 16)
        for k in range(KT):
            self.s["xh_ready"].up(self.nc.scalar.activation(self.xh[:, k], self.x[:, k], ACT.Copy))
        self.wait_consts(act)
        self.act_then(act, self.nc.scalar.activation(self.c_act[:], self.c_act[:], ACT.Silu))

    def dve_start(self, dve, st):
        nc, s = self.nc, self.s
        for n in ("hid", "hid_lo", "z_ready"):
            dve.sem_inc(s[n].sem, PRIMED[n])
        nc.vector.memset(self.zero[:], 0.0).then_inc(self.setup, 1)
        nc.vector.memset(self.ones[:], 1.0 / D).then_inc(self.setup, 1)
        for i, v in enumerate((LN_EPS, 4 * LN_EPS, RMS_EPS, np.pi / 2)):
            nc.vector.memset(self.eps[:, i:i + 1], v).then_inc(self.setup, 1)
        dve.wait_ge(self.x_in, 16)
        for k in range(KT):
            dve.wait_ge(s["xh_ready"].sem, st.at("xh_ready", k + 1))
            s["acts"].up(nc.vector.tensor_tensor(self.xl[:, k], self.x[:, k], self.xh[:, k].bitcast(F32), ALU.subtract))
        self.wait_consts(dve)

    def pe_start(self, pe, st):
        pe.sem_inc(self.s["acc"].sem, PRIMED["acc"])
        pe.wait_ge(self.setup, 6)
        self.wait_consts(pe)

    def pool_start(self, pool, st):
        pool.sem_inc(self.s["w_lo"].sem, PRIMED["w_lo"])

    def dve_norm_sums(self, dve, st, ev):
        nc, s = self.nc, self.s
        for m in range(KT):
            ev(m)
            if m:
                dve.wait_ge(s["z_ready"].sem, st.at("z_ready", m + 1))
                a = self.x[:, 0] if m == 1 else self.zsum[:]
                if m > 1:
                    dve.wait_ge(s["dve_step"].sem, t)
                ins = nc.vector.tensor_tensor(self.zsum[:], a, self.x[:, m], ALU.add)
                if m < KT - 1:
                    t = s["dve_step"].up(ins)
                else:
                    s["zsum_ready"].up(ins)

    def pe_norm(self, pe, st):
        nc, s = self.nc, self.s
        pe.wait_ge(s["zsum_ready"].sem, st.at("zsum_ready", 1))
        s["mean_ready"].up(nc.tensor.matmul(self.ps[:, 0], self.ones[:], self.zsum[:], start=True, stop=True))
        self.pe_squares(pe, st, 0, 1)

    def square_at(self, m, ring):
        return self.sq[:, m % 2] if ring else self.squares[:, m]

    def pair_at(self, p):
        return (self.zsum, self.std)[p % 2]

    def pe_squares(self, pe, st, n, bank):
        s = self.s
        for p in range(PAIRS):
            pe.wait_ge(s["sq_pair"].sem, st.at("sq_pair", PAIRS * n + p + 1))
            s["var_part"].up(self.nc.tensor.matmul(self.ps[:, bank], self.ones[:], self.pair_at(p)[:], start=p == 0, stop=p == PAIRS - 1))

    def act_squares(self, act, st, n, bank, eps, src, before, ring=False):
        nc, s = self.nc, self.s
        for m in range(KT):
            before(m)
            if ring and m >= 2:
                act.wait_ge(s["sq_pair"].sem, st.at("sq_pair", PAIRS * n + m // 2))
            s["sq_ready"].up(nc.scalar.activation(self.square_at(m, ring), src(m), ACT.Square))
        act.wait_ge(s["var_part"].sem, st.at("var_part", PAIRS * (n + 1)))
        s["std_ready"].up(nc.scalar.activation(self.std[:], self.ps[:, bank], ACT.Sqrt, bias=self.eps[:, eps:eps + 1]))

    def dve_square_pair(self, dve, st, n, p, ring=False):
        s = self.s
        dve.wait_ge(s["sq_ready"].sem, st.at("sq_ready", KT * n + 2 * p + 2))
        if p >= 2:
            dve.wait_ge(s["var_part"].sem, st.at("var_part", PAIRS * n + p - 1))
        s["sq_pair"].up(self.nc.vector.tensor_tensor(self.pair_at(p)[:], self.square_at(2 * p, ring), self.square_at(2 * p + 1, ring), ALU.add))

    def splits(self, kind, index):
        return (kind, index) != ("ffn", 2 * DEPTH - 1)

    def act_norm(self, act, st, u, eps):
        nc, s = self.nc, self.s
        self.act_squares(act, st, 0, 1, eps, lambda m: self.x[:, m],
                         lambda m: act.wait_ge(s["dev_ready"].sem, st.at("dev_ready", m + 1)))
        for m in range(KT):
            act.wait_ge(s["t_ready"].sem, st.at("t_ready", m + 1))
            t = s["x_ready"].up(nc.scalar.activation(self.x[:, m], self.x[:, m], ACT.Identity,
                                                     scale=self.ln[:, 0, u, m:m + 1], bias=self.ln[:, 1, u, m:m + 1]))
            if not self.splits(st.kind, st.index):
                continue
            act.wait_ge(s["x_ready"].sem, t)
            s["xh_ready"].up(nc.scalar.activation(self.xh[:, m], self.x[:, m], ACT.Copy))

    def dve_norm(self, dve, st):
        nc, s = self.nc, self.s
        dve.wait_ge(s["mean_ready"].sem, st.at("mean_ready", 1))
        for m in range(KT):
            s["dev_ready"].up(nc.vector.tensor_tensor(self.x[:, m], self.x[:, m], self.ps[:, 0], ALU.subtract))
            if m in (3, 5, 7):
                self.dve_square_pair(dve, st, 0, (m - 3) // 2)
        self.dve_square_pair(dve, st, 0, PAIRS - 1)
        dve.wait_ge(s["std_ready"].sem, st.at("std_ready", 1))
        t = s["dve_step"].up(nc.vector.reciprocal(self.std[:], self.std[:]))
        dve.wait_ge(s["dve_step"].sem, t)
        for m in range(KT):
            s["t_ready"].up(nc.vector.tensor_tensor(self.x[:, m], self.x[:, m], self.std[:], ALU.mult))
            if m and self.splits(st.kind, st.index):
                self.dve_low(dve, st, m - 1)
        if self.splits(st.kind, st.index):
            self.dve_low(dve, st, KT - 1)

    def dve_low(self, dve, st, m):
        s = self.s
        dve.wait_ge(s["xh_ready"].sem, st.at("xh_ready", m + 1))
        s["acts"].up(self.nc.vector.tensor_tensor(self.xl[:, m], self.x[:, m], self.xh[:, m].bitcast(F32), ALU.subtract))

    def stage_ffn(self, n):
        i, half = divmod(n, 2)
        g, u, d = (self.dram[f"ffn{half + 1}_w_{k}"][i] for k in ("gate", "up", "down"))
        pairs = [(w, 0, KT, (0, 256), 256) for w in (g, u)]
        down, k0 = [], 0
        for mp in range(2):
            k0 = 0
            for k in DOWN_PARTS:
                down.append((d, k0, k, (256 * mp, 512), 256))
                k0 += k
        norm = {k: v for k, v in NORM.items() if k not in ("xh_ready", "acts") or self.splits("ffn", n)}
        return add(FFN, norm), [(FT // 2, pairs), (2, down)]

    def memory_ffn(self, own):
        self.hid_h = self.sb("hid_h", [P, FT, T], F32R, own)
        self.hid_l = self.sb("hid_l", [P, FT, T], F32R, own)
        self.sg = self.sb("sg", [P, 2, T], F32, own)
        self.hp = self.sb("hp", [P, 2, T], F32, own)
        self.ada_raw = (self.sb("ada_raw", [P, 2, ADA_GROUP], F32, own), self.stats)

    def pe_ffn(self, pe, st):
        s, c0, ps = self.s, st.chunk0, self.ps
        ada = self.with_ada(st)
        with rolled(pe, FT // 2, {s["acc"]: 4, **({s["ada_mm"]: 1} if ada else {})}) as i:
            for part, (c, freed) in enumerate(((c0, "gate_act"), (c0 + 1, "hid"))):
                self.wait_chunk(pe, c + 2 * i)
                for m in range(2):
                    pe.wait_ge(s[freed].sem, st.at(freed, m - 1) + 2 * i)
                    self.product(pe, c % 2, KT, 256, m * P, ps[:, 2 * part + m], self.x_parts(),
                                 before=self.x_tile(pe, st) if part == m == 0 else None)
            if ada:
                self.pe_ada(pe, i, 7)
        if ada:
            pe.wait_ge(s["ada_out"].sem, FT // 2)
        c1 = c0 + FT
        with rolled(pe, 2, {s["acc"]: 12}) as i:
            for mp in range(2):
                k0 = 0
                for part, k in enumerate(DOWN_PARTS):
                    c = c1 + 3 * mp + part
                    self.wait_chunk(pe, c + 6 * i)
                    pe.wait_ge(s["hid_lo"].sem, st.at("hid_lo", k0 + k))
                    for m in range(2):
                        if part == 0:
                            pe.wait_ge(s["z_ready"].sem, st.at("z_ready", 2 * mp + m - 3) + 4 * i)
                        self.product(pe, c % 2, k, 256, m * P, ps[:, 4 + 2 * mp + m],
                                     ((lambda t, k0=k0: self.hid_h[:, k0 + t, :]), (lambda t, k0=k0: self.hid_l[:, k0 + t, :])),
                                     start=part == 0, stop=part == 2)
                    k0 += k
        if ada:
            self.pe_ada(pe, FT // 2, 3)
        self.pe_norm(pe, st)

    def act_ffn(self, act, st):
        nc, s, c0 = self.nc, self.s, st.chunk0
        ada = self.with_ada(st)
        if ada:
            self.act_ada(act, 0, (0, 1))
        with rolled(act, FT // 2, {s["gate_act"]: 2, s["hid_hi"]: 2}) as i:
            if ada:
                self.act_ada(act, i, (2, 3))
            for m in range(2):
                act.wait_ge(s["acc"].sem, self.acc(c0, m) + 4 * i)
                act.wait_ge(s["hid"].sem, st.at("hid", m - 1) + 2 * i)
                s["gate_act"].up(nc.scalar.activation(self.sg[:, m], self.ps[:, m], ACT.Silu))
            if ada:
                self.act_ada(act, i + 1, (0, 1))
            for m in range(2):
                act.wait_ge(s["hid"].sem, st.at("hid", m + 1) + 2 * i)
                s["hid_hi"].up(nc.scalar.activation(self.hid_h[:, 2 * i + m], self.hp[:, m], ACT.Copy))
        if ada:
            self.act_ada(act, FT // 2, (2, 3))
        self.act_norm(act, st, self.ln_of("ffn", st.index), 1)

    def dve_ffn(self, dve, st):
        nc, s, c0 = self.nc, self.s, st.chunk0
        ada = self.with_ada(st)
        with rolled(dve, FT // 2, {s["hid"]: 2, s["hid_lo"]: 2, **({s["ada_mul"]: KT, s["ada_out"]: 1} if ada else {})}) as i:
            if ada:
                self.dve_ada_sum(dve, i)
            for m in range(2):
                dve.wait_ge(s["acc"].sem, self.acc(c0 + 1, m) + 4 * i)
                dve.wait_ge(s["gate_act"].sem, st.at("gate_act", m + 1) + 2 * i)
                dve.wait_ge(s["hid_lo"].sem, st.at("hid_lo", m - 1) + 2 * i)
                t = s["hid"].up(nc.vector.tensor_tensor(self.hp[:, m], self.sg[:, m], self.ps[:, 2 + m], ALU.mult))
                dve.wait_ge(s["hid"].sem, t)
                dve.wait_ge(s["hid_hi"].sem, st.at("hid_hi", m + 1) + 2 * i)
                s["hid_lo"].up(nc.vector.tensor_tensor(self.hid_l[:, 2 * i + m], self.hp[:, m],
                                                       self.hid_h[:, 2 * i + m].bitcast(F32), ALU.subtract))
            if ada:
                self.dve_ada_out(dve, i, 7)
        c1 = c0 + FT
        if ada:
            self.dve_ada_sum(dve, FT // 2)

        def ev(m):
            dve.wait_ge(s["acc"].sem, self.acc(c1 + 3 * (m // 2) + 2, m % 2))
            s["z_ready"].up(nc.vector.scalar_tensor_tensor(self.x[:, m], self.x[:, m], 2 * ALPHA,
                                                           self.ps[:, 4 + m % 4], ALU.mult, ALU.add))
        self.dve_norm_sums(dve, st, ev)
        if ada:
            self.dve_ada_out(dve, FT // 2, 3)
        self.dve_norm(dve, st)
        if ada:
            self.dve_modulation(dve)

    @staticmethod
    def ln_of(kind, n):
        return {"ffn": [0, 2, 3, 5], "pool": [1], "attn": [4]}[kind][n]

    def dve_then(self, dve, ins):
        dve.wait_ge(self.s["dve_step"].sem, self.s["dve_step"].up(ins))

    def act_then(self, act, ins):
        act.wait_ge(self.s["act_step"].sem, self.s["act_step"].up(ins))

    def out_chunks(self, w):
        return (2, [(w, 0, KT, (0, 512), 256), (w, 0, KT, (256, 512), 256)])

    def pe_out(self, pe, st, c1, xs, before=None):
        with rolled(pe, 2, {self.s["acc"]: 4}) as i:
            for mp in range(2):
                self.wait_chunk(pe, c1 + mp + 2 * i)
                for m in range(2):
                    pe.wait_ge(self.s["z_ready"].sem, st.at("z_ready", 2 * mp + m - 3) + 4 * i)
                    self.product(pe, (c1 + mp) % 2, KT, 256, m * P, self.ps[:, 2 * mp + m], xs,
                                 before=before if mp == m == 0 else None)


    def stage_pool(self, n):
        d = self.dram
        loads = [(d["pool_w_in"][0], 0, KT, (256 * g, 0), 256) for g in range(GROUPS)]
        loads.append((d["pool_w_group"][0].rearrange("g k n -> (g k) n"), 0, KT, (0, 0), 256))
        return add(POOLED, NORM), [(1, loads), self.out_chunks(d["pool_w_out"][0])]

    def memory_pool(self, own):
        w = T + 2 * PAD
        self.padded = self.sb("padded", [P, 2, 2, w], F32, own)
        self.win_a = self.sb("win_a", [P, 2, w], F32, own)
        self.win_b = self.sb("win_b", [P, 2, w], F32, own)
        self.inv_count = self.sb("inv_count", [P, GROUPS, T], F32, own)
        self.mix = self.sb("mix", [P, 2, 2, T], F32, own)
        self.y = self.sb("y", [P, 2, T], F32, own)
        self.y_h = self.sb("y_h", [P, KT, T], F32R, own)
        self.y_l = self.sb("y_l", [P, KT, T], F32R, own)

    def wait_group(self, eng, st, g):
        if g < GROUPS - 1:
            eng.wait_ge(self.s["y_mm"].sem, 2 * g + 2)
        else:
            eng.wait_ge(self.s["acc"].sem, self.acc(st.chunk0 + GROUPS, 1))

    def pe_pool(self, pe, st):
        s, ps = self.s, self.ps
        for g in range(GROUPS):
            c = st.chunk0 + g
            self.wait_chunk(pe, c)
            for m in range(2):
                if g >= 2:
                    pe.wait_ge(s["u_ready"].sem, st.at("u_ready", 2 * g + m - 3))
                self.product(pe, c % 2, KT, 256, m * P, ps[:, 2 * (g % 2) + m], self.x_parts(),
                             before=self.x_tile(pe, st) if g == m == 0 else None)
        c = st.chunk0 + GROUPS
        self.wait_chunk(pe, c)
        for g in range(GROUPS):
            pe.wait_ge(s["mixed_lo"].sem, st.at("mixed_lo", 2 * g + 2))
            for m in range(2):
                if g >= 2:
                    pe.wait_ge(s["y_full"].sem, st.at("y_full", 2 * g + m - 3))
                mm = self.product(pe, c % 2, 2, 256, m * P, ps[:, 4 + 2 * (g % 2) + m],
                                  ((lambda t: self.y_h[:, 2 * g + t]), (lambda t: self.y_l[:, 2 * g + t])),
                                  count=g == GROUPS - 1, t0=2 * g)
                if g < GROUPS - 1:
                    s["y_mm"].up(mm)
        self.pe_out(pe, st, st.chunk0 + GROUPS + 1, ((lambda t: self.y_h[:, t]), (lambda t: self.y_l[:, t])),
                    before=lambda t: pe.wait_ge(s["y_lo"].sem, st.at("y_lo", t + 1)))
        self.pe_norm(pe, st)

    def act_pool(self, act, st):
        nc, s, ps = self.nc, self.s, self.ps
        act.dma_start(self.inv_count[:], self.dram["const_inv_count"].rearrange("a (g t) -> a g t", g=GROUPS)
                      .to_broadcast([P, GROUPS, T])).then_inc(self.tables_in, 16)
        for g in range(GROUPS):
            for m in range(2):
                act.wait_ge(s["acc"].sem, self.acc(st.chunk0 + g, m))
                if g >= 2:
                    act.wait_ge(s["mixed"].sem, st.at("mixed", 2 * g - 2))
                s["u_ready"].up(nc.scalar.activation(self.padded[:, g % 2, m, PAD:PAD + T], ps[:, 2 * (g % 2) + m], ACT.Copy))
            for n in (2 * g, 2 * g + 1):
                act.wait_ge(s["mixed"].sem, st.at("mixed", n + 1))
                s["mixed_hi"].up(nc.scalar.activation(self.y_h[:, n], self.mix[:, g % 2, n % 2], ACT.Copy))
        for n in range(KT):
            self.wait_group(act, st, n // 2)
            if n >= 2:
                act.wait_ge(s["y_lo"].sem, st.at("y_lo", n - 1))
            t = s["y_full"].up(nc.scalar.activation(self.y[:, n % 2], ps[:, 4 + n % 4], ACT.Copy, scale=self.pool_scale[:, n:n + 1]))
            act.wait_ge(s["y_full"].sem, t)
            s["y_hi"].up(nc.scalar.activation(self.y_h[:, n], self.y[:, n % 2], ACT.Copy))
        self.act_norm(act, st, self.ln_of("pool", 0), 0)

    def dve_pool(self, dve, st):
        nc, s, ps = self.nc, self.s, self.ps
        for b in range(2):
            for a in (0, PAD + T):
                self.dve_then(dve, nc.vector.memset(self.padded[:, b, :, a:a + PAD], 0.0))
        for g in range(GROUPS):
            u = self.padded[:, g % 2]
            dve.wait_ge(s["u_ready"].sem, st.at("u_ready", 2 * g + 2))
            if g == 0:
                dve.wait_ge(self.tables_in, self.tables_at(st, "pool"))
            src, w, a, b = u, T + 2 * PAD, self.win_a, self.win_b
            for level in range(g + 1):
                back, ahead = (1, 0) if level == 0 else (1 << (level - 1),) * 2
                lo = 1 << level if level else 1
                hi = w - (0 if level == 0 else lo)
                self.dve_then(dve, nc.vector.tensor_tensor(a[:, :, lo:hi], src[:, :, lo - back:hi - back],
                                                           src[:, :, lo + ahead:hi + ahead], ALU.add))
                src, a, b = a, b, a
            for m in range(2):
                mix = self.mix[:, g % 2, m]
                self.dve_then(dve, nc.vector.tensor_tensor(mix, src[:, m, PAD:PAD + T], self.inv_count[:, g], ALU.mult))
                s["mixed"].up(nc.vector.tensor_tensor(mix, mix, u[:, m, PAD:PAD + T], ALU.subtract))
            for m in range(2):
                n = 2 * g + m
                dve.wait_ge(s["mixed_hi"].sem, st.at("mixed_hi", n + 1))
                s["mixed_lo"].up(nc.vector.tensor_tensor(self.y_l[:, n], self.mix[:, g % 2, m],
                                                         self.y_h[:, n].bitcast(F32), ALU.subtract))
        for n in range(KT):
            dve.wait_ge(s["y_hi"].sem, st.at("y_hi", n + 1))
            s["y_lo"].up(nc.vector.tensor_tensor(self.y_l[:, n], self.y[:, n % 2], self.y_h[:, n].bitcast(F32), ALU.subtract))
        c1 = st.chunk0 + GROUPS + 1

        def ev(m):
            dve.wait_ge(s["acc"].sem, self.acc(c1 + m // 2, m % 2))
            s["z_ready"].up(nc.vector.scalar_tensor_tensor(self.x[:, m], self.x[:, m], ALPHA, ps[:, m % 4], ALU.mult, ALU.add))
        self.dve_norm_sums(dve, st, ev)
        self.dve_norm(dve, st)

    TURN_LAG, OUT_LAG = 2, 3
    Q_SCALE = -E ** -0.5

    def memory_units(self, own, width, ctx_name):
        sb = lambda n, shape: self.sb(ctx_name + n, shape, F32, own)
        self.sc, self.pr, self.pt = (sb(n, [P, 2, width]) for n in ("_scores", "_probs", "_probs_t"))
        self.nb, self.den = sb("_nbias", [P, 4]), sb("_den", [P, 4])
        self.rd = sb("_rden", [P, 2])

    def pe_unit_step(self, pe, st, i, lo, hi, unit, parts):
        nc, s, ps = self.nc, self.s, self.ps
        if lo <= i < hi:
            if i >= lo + 2:
                pe.wait_ge(s["sc_ready"].sem, st.at("sc_ready", parts * (i - 1)))
            for b, c, products in unit(i)["scores"]:
                for j, (q, k) in enumerate(products):
                    mm = nc.tensor.matmul(ps[:, 2 + 2 * (i % 2) + b, c], q, k, start=j == 0, stop=j == len(products) - 1)
            s["scored"].up(mm)
        n = i - self.TURN_LAG
        if lo <= n < hi:
            pe.wait_ge(s["normed"].sem, st.at("normed", n + 1))
            if n > lo:
                pe.wait_ge(s["pt_copied"].sem, st.at("pt_copied", n))
            for j, (b, c) in enumerate(unit(n)["blocks"]):
                mm = nc.tensor.transpose(ps[:, 6 + b, c * P:(c + 1) * P], self.pr[:, n % 2, j * P:(j + 1) * P], self.identity[:])
            s["t_done"].up(mm)
        n = i - self.OUT_LAG
        if lo <= n < hi:
            pe.wait_ge(s["pt_copied"].sem, st.at("pt_copied", n + 1))
            vs = unit(n)["v"]
            for j, v in enumerate(vs):
                mm = nc.tensor.matmul(unit(n)["out"], v, self.pt[:, n % 2, j * P:(j + 1) * P], start=j == 0, stop=j == len(vs) - 1)
            s["pv_done"].up(mm)

    def act_unit_step(self, act, st, i, lo, hi, unit):
        nc, s = self.nc, self.s
        n = i - self.TURN_LAG
        if lo <= n < hi:
            width = unit(n)["width"]
            act.wait_ge(s["t_done"].sem, st.at("t_done", n + 1))
            if n >= lo + 2:
                act.wait_ge(s["pv_done"].sem, st.at("pv_done", n - 1))
            turned = self.ps[:, 6:8].rearrange("p b t -> p (b t)")[:, 0:width]
            s["pt_copied"].up(nc.scalar.activation(self.pt[:, n % 2, 0:width], turned, ACT.Copy))
        if lo <= i < hi:
            width = unit(i)["width"]
            act.wait_ge(s["nbias"].sem, st.at("nbias", i + 1))
            if i >= lo + 2:
                act.wait_ge(s["t_done"].sem, st.at("t_done", i - 1))
            s["probs"].up(nc.scalar.activation(self.pr[:, i % 2, 0:width], self.sc[:, i % 2, 0:width], ACT.Exp,
                                               scale=-1.0, bias=self.nb[:, i % 4:i % 4 + 1],
                                               accum_out=self.den[:, i % 4:i % 4 + 1]))

    def dve_unit_step(self, dve, st, i, lo, hi, unit):
        nc, s = self.nc, self.s
        if lo <= i < hi:
            u = unit(i)
            dve.wait_ge(s["scored"].sem, st.at("scored", i + 1))
            if i >= lo + 2:
                dve.wait_ge(s["probs"].sem, st.at("probs", i - 1))
            for b, src, dst, bias, factor in u["biases"]:
                in1 = self.ps[:, 2 + 2 * (i % 2) + b, src]
                t = s["sc_ready"].up(nc.vector.scalar_tensor_tensor(self.sc[:, i % 2, dst], bias, factor, in1, ALU.mult, ALU.add))
            dve.wait_ge(s["sc_ready"].sem, t)
            nb = self.nb[:, i % 4:i % 4 + 1]
            s["nbias"].up(nc.vector.tensor_reduce(nb, self.sc[:, i % 2, 0:u["width"]], AX.X, ALU.min))
        n = i - 1
        if lo <= n < hi:
            dve.wait_ge(s["probs"].sem, st.at("probs", n + 1))
            rd, pr = self.rd[:, n % 2:n % 2 + 1], self.pr[:, n % 2, 0:unit(n)["width"]]
            self.dve_then(dve, nc.vector.reciprocal(rd, self.den[:, n % 4:n % 4 + 1]))
            s["normed"].up(nc.vector.tensor_scalar(pr, pr, rd, None, ALU.mult))

    def stage_attn(self, n):
        w, loads = self.dram["attn_w_qkv"][0], []
        for quad in range(QUADS):
            loads += [(w, 0, KT, (g * 3072 + part * 1024 + quad * 256, 0), 256) for g in range(3) for part in range(3)]
        return add(ATTN, NORM), [(1, loads), self.out_chunks(self.dram["attn_w_out"][0])]

    def memory_attn(self, own):
        sb = self.sb
        self.at_qk0 = sb("at_qk0", [P, 2, 2, T], F32R, own)
        self.at_qk0_l = sb("at_qk0_l", [P, 2, 2, T], F32R, own)
        self.at_q = sb("at_q", [P, 2, 2, T], F32, own)
        self.at_k = sb("at_k", [P, 2, 2, T], F32, own)
        self.at_v = sb("at_v", [P, 3, 4, 256], F32, own)
        self.dist0 = (self.sq, sb("dist0", [P, 2, T], F32, own))
        self.dist12 = sb("dist12", [P, 2, P], F32, own)
        self.at_oh = sb("at_oh", [P, KT, T], F32R, own)
        self.at_ol = sb("at_ol", [P, KT, T], F32R, own)
        with ExitStack() as units:
            self.memory_units(units, 768, "attn")
            self.attn_units = (self.sc, self.pr, self.pt, self.nb, self.den, self.rd)

    def attn_unit(self, n):
        quad, hh, r = n // 16, n // 4 % 4, n % 4
        tile, part = hh // 2, slice(64 * (hh % 2), 64 * (hh % 2) + 64)
        own = slice(r * P, (r + 1) * P)
        (qh, ql), (kh, kl) = ((self.at_qk0[part, a, tile], self.at_qk0_l[part, a, tile]) for a in range(2))
        qh, ql = qh[:, own], ql[:, own]
        q, k = ([None] + [buf[part, g, tile] for g in range(2)] for buf in (self.at_q, self.at_k))
        cols = slice(hh * E, (hh + 1) * E)
        slope = lambda g: self.slopes[:, quad * 12 + g * 4 + hh:quad * 12 + g * 4 + hh + 1]
        v = [self.at_v[:, 0, kt, cols] for kt in range(4)] + [self.at_v[:, g, r, cols] for g in (1, 2)]
        return dict(
            scores=[(0, slice(0, T), ((qh, kh), (qh, kl), (ql, kh)))] +
                   [(1, slice((g - 1) * P, g * P), ((q[g][:, own], k[g][:, own]),)) for g in (1, 2)],
            biases=[(0, slice(0, T), slice(0, T), self.dist0[r // 2][:, r % 2], slope(0))] +
                   [(1, slice((g - 1) * P, g * P), slice(T + (g - 1) * P, T + g * P), self.dist12[:, g - 1], slope(g)) for g in (1, 2)],
            width=T + 2 * P, blocks=[(0, j) for j in range(4)] + [(1, 0), (1, 1)], v=v, out=self.ps[part, tile, own])

    def use_attn_units(self):
        self.sc, self.pr, self.pt, self.nb, self.den, self.rd = self.attn_units

    @staticmethod
    def by_residue(ap):
        return ap.rearrange("q (p r) -> q r p", r=4)

    def pe_attn(self, pe, st):
        nc, s, ps = self.nc, self.s, self.ps
        self.use_attn_units()
        for quad in range(QUADS):
            for j in range(9):
                c = st.chunk0 + 9 * quad + j
                self.wait_chunk(pe, c)
                for m in range(2):
                    n = 18 * quad + 2 * j + m
                    if n >= 2:
                        pe.wait_ge(s["lin_ev"].sem, st.at("lin_ev", n - 1))
                    if j in (1, 2):
                        pe.wait_ge(s["qk_low"].sem, st.at("qk_low", 4 * quad + 2 * (j - 1) + m + 1))
                    if j == 0 and quad:
                        pe.wait_ge(s["o_lo"].sem, st.at("o_lo", 2 * (quad - 1) + m + 1))
                    if j % 3 < 2:
                        self.product(pe, c % 2, KT, 256, m * P, ps[:, m], self.x_parts(),
                                     before=self.x_tile(pe, st) if n == 0 else None)
                    else:
                        self.values(pe, c % 2, 256, 0, 256, m, [self.by_residue(self.xh[:, t]) for t in range(KT)],
                                    [self.by_residue(self.xl[:, t]) for t in range(KT)])
            pe.wait_ge(s["lin_ev"].sem, st.at("lin_ev", 18 * (quad + 1)))
            lo, hi = 16 * quad, 16 * quad + 16
            for i in range(lo, hi + self.OUT_LAG):
                self.pe_unit_step(pe, st, i, lo, hi, self.attn_unit, 3)
        pe.wait_ge(s["o_lo"].sem, st.at("o_lo", 2 * QUADS))
        self.pe_out(pe, st, st.chunk0 + 9 * QUADS, ((lambda t: self.at_oh[:, t]), (lambda t: self.at_ol[:, t])))
        self.pe_norm(pe, st)

    def values(self, pe, slot, stride, c0, width, m, xh, xl):
        for r in (2 * m, 2 * m + 1):
            out = self.ps[:, m, (r % 2) * 256:(r % 2) * 256 + width]
            for t in range(KT):
                w = slice(t * stride + c0, t * stride + c0 + width)
                for q, (x, b) in enumerate(((xh, self.wh), (xh, self.wl), (xl, self.wh))):
                    mm = self.nc.tensor.matmul(out, x[t][:, r], b[:, slot, w], start=t == 0 and q == 0, stop=t == KT - 1 and q == 2)
        self.s["acc"].up(mm)

    def act_attn(self, act, st):
        nc, s, ps = self.nc, self.s, self.ps
        self.use_attn_units()
        dist0 = self.dram["const_dist0"].rearrange("p (a r t) -> p a r t", a=2, r=2)
        for a in range(2):
            act.dma_start(self.dist0[a][:], dist0[:, a]).then_inc(self.tables_in, 16)
        act.dma_start(self.dist12[:], self.dram["const_dist12"].rearrange("p (a t) -> p a t", a=2)).then_inc(self.tables_in, 16)
        for quad in range(QUADS):
            for j in range(9):
                g, part = divmod(j, 3)
                for m in range(2):
                    act.wait_ge(s["acc"].sem, self.acc(st.chunk0 + 9 * quad + j, m))
                    if part < 2:
                        buf = self.at_qk0[:, part, m] if g == 0 else (self.at_q, self.at_k)[part][:, g - 1, m]
                        dst = buf.rearrange("q (r p) -> q r p", r=4)
                        scale = self.Q_SCALE if part == 0 else 1.0
                        src = self.by_residue(ps[:, m])
                    else:
                        dst = self.at_v[:, g, 2 * m:2 * m + 2]
                        src = ps[:, m].rearrange("q (r n) -> q r n", r=2)
                        scale = 1.0
                    s["lin_ev"].up(nc.scalar.activation(dst, src, ACT.Copy, scale=scale))
            lo, hi = 16 * quad, 16 * quad + 16
            for i in range(lo, hi + self.OUT_LAG):
                self.act_unit_step(act, st, i, lo, hi, self.attn_unit)
            for tile in range(2):
                act.wait_ge(s["pv_done"].sem, st.at("pv_done", lo + 8 * tile + 8))
                s["o_hi"].up(nc.scalar.activation(self.at_oh[:, 2 * quad + tile], ps[:, tile], ACT.Copy))
        self.act_norm(act, st, self.ln_of("attn", 0), 0)

    def dve_attn(self, dve, st):
        nc, s, ps = self.nc, self.s, self.ps
        self.use_attn_units()
        dve.wait_ge(self.tables_in, self.tables_at(st, "attn"))
        for quad in range(QUADS):
            for j in range(2):
                for m in range(2):
                    dve.wait_ge(s["lin_ev"].sem, st.at("lin_ev", 18 * quad + 2 * j + m + 1))
                    low, high = (b.rearrange("q (r p) -> q r p", r=4) for b in (self.at_qk0_l[:, j, m], self.at_qk0[:, j, m]))
                    scale = self.Q_SCALE if j == 0 else 1.0
                    s["qk_low"].up(nc.vector.scalar_tensor_tensor(low, self.by_residue(ps[:, m]), scale, high.bitcast(F32),
                                                                  ALU.mult, ALU.subtract))
            lo, hi = 16 * quad, 16 * quad + 16
            for i in range(lo, hi + self.OUT_LAG):
                self.dve_unit_step(dve, st, i, lo, hi, self.attn_unit)
            for tile in range(2):
                n = 2 * quad + tile
                dve.wait_ge(s["o_hi"].sem, st.at("o_hi", n + 1))
                s["o_lo"].up(nc.vector.tensor_tensor(self.at_ol[:, n], ps[:, tile], self.at_oh[:, n].bitcast(F32), ALU.subtract))
        c1 = st.chunk0 + 9 * QUADS

        def ev(m):
            dve.wait_ge(s["acc"].sem, self.acc(c1 + m // 2, m % 2))
            x = self.by_residue(self.x[:, m])
            s["z_ready"].up(nc.vector.scalar_tensor_tensor(x, x, ALPHA, ps[:, m % 4].rearrange("q (r p) -> q r p", r=4), ALU.mult, ALU.add))
        self.dve_norm_sums(dve, st, ev)
        self.dve_norm(dve, st)

    TABLES = dict(pool=1, attn=3, mixer=8)

    def tables_at(self, st, kind, later=0):
        n = sum(self.TABLES.get(o.kind, 0) for o in self.stages[:self.stages.index(st)])
        return 16 * (n + self.TABLES[kind] - later)

    def with_ada(self, st):
        return self.mixes and st.index == 0

    def act_ada(self, act, j, pieces):
        w = self.dram["ada_w_2"].rearrange("(k p) n -> p k n", p=P)
        for q in pieces:
            if q >= 2 or not isinstance(j, int):
                act.wait_ge(self.s["ada_mul"].sem, KT * j + 2 * (q - 1))
            src = w[:, 2 * q:2 * q + 2, bass.ds(ADA_GROUP * j, ADA_GROUP)]
            act.dma_start(self.ada_raw[q % 2][:], src).then_inc(self.ada_in[q % 2], 16)

    def dve_ada_sum(self, dve, j):
        s, v = self.s, self.nc.vector
        total = self.sq[:, 0]
        dve.wait_ge(s["act_step"].sem, 1)
        for k in range(KT):
            q, part = divmod(k, 2)
            if part == 0:
                dve.wait_ge(self.ada_in[q % 2], 32 * j + 16 * (q // 2 + 1))
            raw, c = self.ada_raw[q % 2][:, part], self.c_act[:, k:k + 1]
            if k == 0:
                ins = v.tensor_scalar(total, raw, c, None, ALU.mult)
            else:
                dve.wait_ge(s["ada_mul"].sem, t)
                ins = v.scalar_tensor_tensor(total, raw, c, total, ALU.mult, ALU.add)
            t = s["ada_mul"].up(ins)

    def pe_ada(self, pe, j, bank):
        s = self.s
        pe.wait_ge(s["ada_mul"].sem, KT * j + KT)
        for m in range(ADA_GROUP // P):
            mm = self.nc.tensor.matmul(self.ps[:, bank, m:m + 1], self.sq[:, 0, m * P:(m + 1) * P], self.ones[:, 0:1], start=True, stop=True)
        s["ada_mm"].up(mm)

    def dve_ada_out(self, dve, j, bank):
        s, n = self.s, ADA_GROUP // P
        dve.wait_ge(s["ada_mm"].sem, j + 1)
        mod, b = (a[:].rearrange("p l n -> p (l n)")[:, bass.ds(n * j, n)] for a in (self.mod, self.ada_b))
        s["ada_out"].up(self.nc.vector.scalar_tensor_tensor(mod, self.ps[:, bank, 0:n], float(D), b, ALU.mult, ALU.add))

    def dve_modulation(self, dve):
        nc, s, mod = self.nc, self.s, self.mod
        dve.wait_ge(s["ada_out"].sem, FT // 2 + 1)
        scale, gate = mod[:, :, KT:2 * KT], mod[:, :, 2 * KT:3 * KT]
        s["mod_ready"].up(nc.vector.scalar_tensor_tensor(scale, scale, 1.0, self.norms[:, 0], ALU.add, ALU.mult))
        s["mod_ready"].up(nc.vector.tensor_tensor(gate, gate, self.norms[:, 1], ALU.mult))

    def stage_mixer(self, n):
        d = self.dram
        w = d["w_in_2"][n]
        col = dict(idx_q=IDX_Q, dsa_q0=DSA_Q, dsa_q1=DSA_Q + 256, dsa_kv=DSA_KV, dsa_g0=DSA_G, dsa_g1=DSA_G + 256,
                   ret_q=RET_Q, ret_k=RET_K, ret_v0=RET_V, ret_v1=RET_V + 256, ret_g0=RET_G, ret_g1=RET_G + 256,
                   gla_q=GLA_Q, gla_k=GLA_K, gla_v0=GLA_V, gla_v1=GLA_V + 256, gla_g0=GLA_G, gla_g1=GLA_G + 256)
        loads, self.mixer_chunk = [], {}
        for name in MIXER_ORDER:
            self.mixer_chunk[name] = len(loads)
            if name in col:
                loads.append((w, 0, KT, (col[name], 0), 256))
            elif name in ("idx_k", "gla_a"):
                loads.append((w, 0, KT, ({"idx_k": IDX_K, "gla_a": GLA_A}[name], 0), P))
            elif name == "out":
                loads += [(d["w_out_2"][n], 0, KT, (256 * mp, 0), 256) for mp in range(4)]
            else:
                b = ("mix_ret", "mix_dsa", "mix_gla").index(name)
                br = d[("w_br_ret_2", "w_br_dsa_2", "w_br_gla_2")[b]][n]
                gates = [(w, 0, KT, (MERGE + b * D + 256 * mp, 0), 256) for mp in range(4)]
                branch = [(br, 0, 4, (512 * half, 0), 512) for half in range(2)]
                loads += [gates[0], branch[0], gates[1], branch[1], gates[2], gates[3]]
        return MIXER, [(1, loads)]

    def memory_mixer(self, own):
        sb = self.sb
        self.mx_y = sb("mx_y", [P, KT, T], F32, own)
        self.mx_g = sb("mx_g", [P, 4, T], F32, own)
        self.rope_t = sb("rope_t", [P, 2, 2, T], F32, own)
        self.pos = sb("pos", [P, T], I32, own)
        self.freq = sb("freq", [P, 2], F32, own)
        self.swap = sb("swap", [P, 2, P], F32, own)
        self.causal = sb("causal", [P, P], F32, own)
        self.masks = sb("masks", [P, 8, P], I32, own)
        self.lr_w = sb("lr_w", [16, 256], F32, own)
        self.mx_sg = sb("mx_sg", [P, 2, T], F32, own)
        self.mx_t = sb("mx_t", [P, 2, T], F32, own)
        self.br_h = sb("br_h", [P, 4, T], F32R, own)
        with ExitStack() as a:
            self.br_free = sb("br_free", [P, 4, T], F32, a)
        self.br_l = sb("br_l", [P, 4, T], F32R, own)
        with ExitStack() as a:
            self.mx_h = sb("mx_h", [P, KT, T], F32, a)
        with ExitStack() as a:
            with ExitStack() as b:
                self.iq = sb("iq", [P, 2, T], F32, b)
            self.kd = sb("kd", [P, 2, T], F32, a)
            self.ik = sb("ik", [P, T], F32, a)
            self.dq = sb("dq", [P, 4, T], F32, a)
            self.dk = sb("dk", [P, T], F32, a)
        for b in ("ret", "gla"):
            with ExitStack() as a:
                qkv = [sb(b + "_q", [P, 2, T], F32, a), sb(b + "_k", [P, 2, T], F32, a), sb(b + "_v", [P, 4, 512], F32, a)]
            if b == "ret":
                self.rq, self.rk, self.rv = qkv
            else:
                self.gq, self.gk, self.gv = qkv
        sb("mx_region", [P, KT * T], F32, own)
        with ExitStack() as a:
            self.dv = sb("dv", [P, 4, P], F32, a)
            self.iw = sb("iw", [P, 4, 4], F32, a)
            self.score = sb("score", [P, 128 * (2 + 3 + 4)], F32, a)
            self.top8 = sb("top8", [P, 8], F32, a)
            self.memory_units(a, T, "dsa")
            self.dsa_units = (self.sc, self.pr, self.pt, self.nb, self.den, self.rd)
        with ExitStack() as a:
            self.decay = sb("decay", [P, 4, T], F32, a)
            self.st = sb("st", [P, 2, T], F32, a)
            self.hs_ret = sb("hs_ret", [P, 2, T], F32, a)
        with ExitStack() as a:
            gqe, gke = (sb(n, [P, T], F32, a) for n in ("gqe", "gke"))
            with ExitStack() as b:
                self.ga = sb("ga", [16, 2, T], F32, b)
            self.gf = sb("gf", [P, T], F32, a)
            self.gr = sb("gr", [P, T], F32, a)
            ge = sb("ge", [P, T], F32, a)
            self.ge = (ge, self.br_free[:, 3])
            self.gqe, self.gke = (gqe, self.mx_sg[:, 0]), (gke, self.mx_sg[:, 1])
            self.sd = sb("sd", [P, 2, T], F32, a)
            self.so = sb("so", [P, 2, 6 * P], F32, a)

    def lin(self, name):
        n = 0
        for o in MIXER_ORDER:
            if o == name:
                return n
            n += 8 if o.startswith("mix_") or o == "out" else 2

    def half_of(self, name, mp, m):
        return self.lin(name) + 2 * mp + m

    def x_tiles(self):
        return ([a[:, t].rearrange("q (r p) -> q r p", r=TT) for t in range(KT)] for a in (self.xh, self.xl))

    def pe_project(self, pe, st, name, kind=("t", "t"), mp=0, at=0, before=None):
        s, ps = self.s, self.ps
        c = st.chunk0 + self.mixer_chunk[name] + at
        self.wait_chunk(pe, c)
        width = P if name in ("idx_k", "gla_a") else 256
        for m in range(2):
            n = self.half_of(name, mp, m)
            pe.wait_ge(s["lin_ev"].sem, st.at("lin_ev", max(n - 1, 0)))
            if kind[m] == "t":
                self.product(pe, c % 2, KT, width, m * P, ps[:, m], self.x_parts(), before=before if m == 0 else None)
            elif kind[m] == "part":
                for t in range(4 * m, 4 * m + 4):
                    for q, (a, b) in enumerate(((self.wh, self.xh), (self.wh, self.xl), (self.wl, self.xh))):
                        mm = self.nc.tensor.matmul(ps[:, m], a[:, c % 2, t * P:(t + 1) * P], b[:, t], start=t == 4 * m and q == 0,
                                                   stop=t == 4 * m + 3 and q == 2)
                s["acc"].up(mm)
            elif kind[m] == "turn":
                pe.wait_ge(s["lin_ev"].sem, st.at("lin_ev", n))
                rows = slice(64, 96)
                for r in range(TT):
                    mm = self.nc.tensor.transpose(ps[:, m, r * 32:(r + 1) * 32], self.ik[rows, r * P:(r + 1) * P], self.identity[rows, rows])
                s["acc"].up(mm)
            elif kind[m] == "v":
                self.values(pe, c % 2, 256, 0, 256, m, *self.x_tiles())
            else:
                c0, w = kind[m]
                xh, xl = self.x_tiles()
                for r in range(TT):
                    for t in range(KT):
                        cols = slice(t * width + c0, t * width + c0 + w)
                        for q, (x, b) in enumerate(((xh, self.wh), (xh, self.wl), (xl, self.wh))):
                            mm = self.nc.tensor.matmul(ps[:, m, r * w:(r + 1) * w], x[t][:, r], b[:, c % 2, cols],
                                                       start=t == 0 and q == 0, stop=t == KT - 1 and q == 2)
                s["acc"].up(mm)

    def act_project(self, act, st, name, dsts, func=ACT.Copy, scale=(1.0, 1.0), srcs=None, mp=0, at=0):
        c = st.chunk0 + self.mixer_chunk[name] + at
        for m in range(2):
            act.wait_ge(self.s["acc"].sem, self.acc(c, m))
            src = srcs[m] if srcs else self.ps[:, m]
            self.s["lin_ev"].up(self.nc.scalar.activation(dsts[m], src, func, scale=scale[m]))

    def dve_squares(self, dve, st, n, ring):
        for p in range(PAIRS):
            self.dve_square_pair(dve, st, n, p, ring)
        dve.wait_ge(self.s["std_ready"].sem, st.at("std_ready", n + 1))
        self.dve_then(dve, self.nc.vector.reciprocal(self.std[:], self.std[:]))

    ROPE_ORDER = ("iq0", "iq1", "ik", "dq0", "dq1", "dq2", "dq3", "dk", "rq0", "rq1", "rk0", "rk1")

    def rope_tile(self, name):
        where = dict(iq=(self.iq, 1, "idx_q"), dq=(self.dq, 1, "dsa_q0"), rq=(self.rq, 0, "ret_q"), rk=(self.rk, 0, "ret_k"))
        if name == "ik":
            return self.ik[:], 1, self.lin("idx_k")
        if name == "dk":
            return self.dk[:], 1, self.lin("dsa_kv")
        buf, table, chunk = where[name[:2]]
        return buf[:, int(name[2])], table, self.lin(chunk) + int(name[2])

    def pe_ropes(self, pe, st, names):
        s = self.s
        for name in names:
            n = self.ROPE_ORDER.index(name)
            src, table, half = self.rope_tile(name)
            pe.wait_ge(s["lin_ev"].sem, st.at("lin_ev", half + 1))
            if n >= 2:
                pe.wait_ge(s["rope_done"].sem, st.at("rope_done", n - 1))
            s["rot"].up(self.nc.tensor.matmul(self.ps[:, 4 + n % 2], self.swap[:, table], src, start=True, stop=True))

    def dve_ropes(self, dve, st, names):
        nc, s = self.nc, self.s
        for name in names:
            n = self.ROPE_ORDER.index(name)
            buf, table, _ = self.rope_tile(name)
            dve.wait_ge(s["rot"].sem, st.at("rot", n + 1))
            self.dve_then(dve, nc.vector.tensor_tensor(self.mx_t[:, 0], self.ps[:, 4 + n % 2], self.rope_t[:, table, 1], ALU.mult))
            self.dve_then(dve, nc.vector.tensor_tensor(buf, buf, self.rope_t[:, table, 0], ALU.mult))
            t = s["rope_done"].up(nc.vector.tensor_tensor(buf, buf, self.mx_t[:, 0], ALU.add))
            dve.wait_ge(s["rope_done"].sem, t)

    def dve_angles(self, dve, st, table):
        if st.index_in_kind:
            return
        nc, s = self.nc, self.s
        v = nc.vector
        dve.wait_ge(self.tables_in, self.tables_at(st, "mixer", later=1))
        ang, n = self.mx_t[:, 0], self.mx_t[:, 1]
        self.dve_then(dve, v.tensor_copy(n, self.pos[:]))
        self.dve_then(dve, v.tensor_scalar(ang, n, self.freq[:, table:table + 1], None, ALU.mult))
        out = self.rope_t[:, table, 1]
        src = ang
        for parts in ((TWO_PI_A, TWO_PI_B, TWO_PI_C), (TWO_PI_A, TWO_PI_B + TWO_PI_C)):
            self.dve_then(dve, v.tensor_scalar(n, src, 1 / (2 * np.pi), ROUND, ALU.mult, ALU.add))
            self.dve_then(dve, v.tensor_scalar(n, n, -ROUND, None, ALU.add))
            for part in parts:
                self.dve_then(dve, v.scalar_tensor_tensor(out, n, -part, src, ALU.mult, ALU.add))
                src = out
        s["angles"].up(v.tensor_scalar(out, out, PI_SAFE, -PI_SAFE, ALU.min, ALU.max))

    def act_waves(self, act, st, table):
        nc = self.nc
        if st.index_in_kind:
            return
        act.wait_ge(self.s["angles"].sem, 2 - table)
        cos, ang = self.rope_t[:, table, 0], self.rope_t[:, table, 1]
        self.act_then(act, nc.scalar.activation(cos, ang, ACT.Abs))
        self.s["waves"].up(nc.scalar.activation(cos, cos, ACT.Sin, scale=-1.0, bias=self.eps[:, 3:4]))
        self.s["waves"].up(nc.scalar.activation(ang, ang, ACT.Sin))

    SCORE_AT = {1: 0, 2: 256, 3: 640}

    def index_units(self):
        for n in range(INDEX_UNITS):
            yield n, n // 4 + 1, n % 4

    def pe_index(self, pe, st):
        nc, s = self.nc, self.s
        pe.wait_ge(s["rope_done"].sem, st.at("rope_done", 3))
        pe.wait_ge(s["ikd_ready"].sem, st.at("ikd_ready", 1))
        for n, qt, h in self.index_units():
            part = slice(64 * (h % 2), 64 * (h % 2) + 64)
            if n >= 2:
                pe.wait_ge(s["idx_relu"].sem, st.at("idx_relu", n - 1))
            width = (qt + 1) * P
            s["idx_mm"].up(nc.tensor.matmul(self.ps[:, 6 + n % 2, 0:width], self.iq[part, h // 2, qt * P:(qt + 1) * P],
                                            self.ik[part, 0:width], start=True, stop=True))

    def act_index(self, act, st):
        nc, s = self.nc, self.s
        for n, qt, h in self.index_units():
            width = (qt + 1) * P
            act.wait_ge(s["idx_mm"].sem, st.at("idx_mm", n + 1))
            if n >= 2:
                act.wait_ge(s["idx_acc"].sem, st.at("idx_acc", n - 1))
            s["idx_relu"].up(nc.scalar.activation(self.sc[:, n % 2, 0:width], self.ps[:, 6 + n % 2, 0:width], ACT.Relu, scale=E ** -0.5))

    def dve_index(self, dve, st):
        nc, s = self.nc, self.s
        dve.wait_ge(s["lin_ev"].sem, st.at("lin_ev", self.lin("idx_k") + 2))
        for n, qt, h in self.index_units():
            width = (qt + 1) * P
            at = self.SCORE_AT[qt]
            out, w = self.score[:, at:at + width], self.iw[:, qt, h:h + 1]
            dve.wait_ge(s["idx_relu"].sem, st.at("idx_relu", n + 1))
            if h == 0:
                ins = nc.vector.tensor_scalar(out, self.sc[:, n % 2, 0:width], w, 0.0, ALU.mult, ALU.add)
            else:
                dve.wait_ge(s["idx_acc"].sem, t)
                ins = nc.vector.scalar_tensor_tensor(out, self.sc[:, n % 2, 0:width], w, out, ALU.mult, ALU.add)
            t = s["idx_acc"].up(ins)
            if h == 3:
                dve.wait_ge(s["idx_acc"].sem, t)
                last = self.score[:, at + qt * P:at + width]
                self.dve_then(dve, nc.vector.tensor_tensor(last, last, self.causal[:], ALU.add))

    def dve_choose_round(self, dve, qt):
        v = self.nc.vector
        score = self.score[:, self.SCORE_AT[qt]:self.SCORE_AT[qt] + (qt + 1) * P]
        self.dve_then(dve, v.max(self.top8[:], score))
        self.dve_then(dve, v.match_replace(score, self.top8[:], score, TAKEN))

    def dve_choose_biases(self, dve, qt):
        score = self.score[:, self.SCORE_AT[qt]:self.SCORE_AT[qt] + (qt + 1) * P]
        self.dve_then(dve, self.nc.vector.tensor_scalar(score, score, -1e35, BIG, ALU.is_ge, ALU.mult))

    DSA_BANKS = (1, 3, 5, 7)

    def dsa_unit(self, n):
        qt, h = divmod(n, 8)
        part = slice(64 * (h % 2), 64 * (h % 2) + 64)
        kv, width = h // 4, (qt + 1) * P
        bias = self.causal[:] if qt == 0 else self.score[:, self.SCORE_AT[qt]:self.SCORE_AT[qt] + width]
        return dict(scores=[(0, slice(0, width), ((self.dq[part, h // 2, qt * P:(qt + 1) * P], self.kd[part, kv, 0:width]),))],
                    biases=[(0, slice(0, width), slice(0, width), bias, -1.0 if qt == 0 else 1.0)],
                    width=width, blocks=[(0, j) for j in range(qt + 1)],
                    v=[self.dv[:, j, kv * 64:kv * 64 + 64] for j in range(qt + 1)], out=self.ps[part, self.DSA_BANKS[h // 2], qt * P:(qt + 1) * P])

    def use_dsa_units(self):
        self.sc, self.pr, self.pt, self.nb, self.den, self.rd = self.dsa_units

    def act_branch_hi(self, act, st, n):
        s = self.s
        act.wait_ge(s["br_full"].sem, st.at("br_full", n + 1))
        s["br_hi"].up(self.nc.scalar.activation(self.br_h[:, n % 4], self.mx_t[:, n % 2], ACT.Copy))

    def dve_branch_lo(self, dve, st, n):
        s = self.s
        dve.wait_ge(s["br_hi"].sem, st.at("br_hi", n + 1))
        s["br_lo"].up(self.nc.vector.tensor_tensor(self.br_l[:, n % 4], self.mx_t[:, n % 2], self.br_h[:, n % 4].bitcast(F32), ALU.subtract))

    def mix_chunk(self, st, name, mp, branch):
        return st.chunk0 + self.mixer_chunk[name] + ((1, 3)[mp // 2] if branch else (0, 2, 4, 5)[mp])

    def mix_bank(self, n):
        return 2 + n % 6

    def pe_mix(self, pe, st, b, name):
        s, ps = self.s, self.ps

        def gates(mp):
            self.pe_project(pe, st, name, mp=mp, at=self.mix_chunk(st, name, mp, False) - st.chunk0 - self.mixer_chunk[name])

        def branch(half):
            c = self.mix_chunk(st, name, 2 * half, True)
            self.wait_chunk(pe, c)
            if half == 0:
                pe.wait_ge(s["br_lo"].sem, st.at("br_lo", 4 * b + 4))
            for q in range(4):
                n = 4 * half + q
                if n >= 6:
                    pe.wait_ge(s["mixed"].sem, st.at("mixed", 8 * b + n - 5))
                self.product(pe, c % 2, 4, 512, q * P, ps[:, self.mix_bank(n)],
                             ((lambda t: self.br_h[:, t]), (lambda t: self.br_l[:, t])), count=q % 2 == 1)
        gates(0)
        branch(0)
        gates(1)
        branch(1)
        gates(2)
        gates(3)

    def act_mix(self, act, st, b, name):
        nc, s = self.nc, self.s
        for mp in range(4):
            for m in range(2):
                n = 8 * b + 2 * mp + m
                act.wait_ge(s["acc"].sem, self.acc(self.mix_chunk(st, name, mp, False), m))
                act.wait_ge(s["mixed"].sem, st.at("mixed", max(n - 1, 0)))
                s["lin_ev"].up(nc.scalar.activation(self.mx_sg[:, m], self.ps[:, m], ACT.Sigmoid))

    def dve_mix(self, dve, st, b, name):
        nc, s = self.nc, self.s
        for mp in range(4):
            for m in range(2):
                n = 2 * mp + m
                dve.wait_ge(s["acc"].sem, self.acc(self.mix_chunk(st, name, mp, True), mp % 2))
                dve.wait_ge(s["lin_ev"].sem, st.at("lin_ev", self.half_of(name, mp, m) + 1))
                y = self.mx_y[:, n]
                out = y if b == 0 else self.mx_sg[:, m]
                ins = nc.vector.tensor_tensor(out, self.mx_sg[:, m], self.ps[:, self.mix_bank(n)], ALU.mult)
                if b:
                    self.dve_then(dve, ins)
                    ins = nc.vector.tensor_tensor(y, y, self.mx_sg[:, m], ALU.add)
                s["mixed"].up(ins)

    def act_head_square(self, act, st, n):
        s = self.s
        act.wait_ge(s["head_done"].sem, st.at("head_done", n + 1))
        s["hsq"].up(self.nc.scalar.activation(self.sq[:, n % 2], self.ps[:, 6 + n % 2], ACT.Square))

    def head_std(self, n):
        return (self.hs_ret if n < 4 else self.stats)[:, n % 2]

    def var_bank(self, n):
        return (2 if n < 4 else 4) + n % 2

    def act_head_std(self, act, st, n):
        s = self.s
        act.wait_ge(s["hvar"].sem, st.at("hvar", n + 1))
        s["hstd"].up(self.nc.scalar.activation(self.head_std(n), self.ps[:, self.var_bank(n)], ACT.Sqrt, scale=float(D // P),
                                               bias=self.eps[:, 2:3]))

    def act_head_rest(self, act, st, n):
        self.act_head_std(act, st, n)
        self.act_branch_hi(act, st, 4 + n)

    def pe_head(self, pe, st, n):
        s = self.s
        pe.wait_ge(s["hsq"].sem, st.at("hsq", n + 1))
        s["hvar"].up(self.nc.tensor.matmul(self.ps[:, self.var_bank(n)], self.ones[:], self.sq[:, n % 2], start=True, stop=True))

    def dve_head_factor(self, dve, st, n):
        dve.wait_ge(self.s["hstd"].sem, st.at("hstd", n + 1))
        hs = self.head_std(n)
        self.dve_then(dve, self.nc.vector.reciprocal(hs, hs))

    def dve_head_gate(self, dve, st, n):
        nc, s, hs = self.nc, self.s, self.head_std(n)
        self.dve_then(dve, nc.vector.tensor_tensor(hs, hs, self.ps[:, 6 + n % 2], ALU.mult))
        s["br_full"].up(nc.vector.tensor_tensor(self.mx_t[:, n % 2], hs, self.mx_g[:, n % 4], ALU.mult))

    def dve_head(self, dve, st, n):
        self.dve_head_factor(dve, st, n)
        self.dve_head_gate(dve, st, n)
        self.dve_branch_lo(dve, st, 4 + n)

    def pe_retention(self, pe, st):
        nc, s, ps = self.nc, self.s, self.ps
        pe.wait_ge(s["rope_done"].sem, st.at("rope_done", ROPES))
        pe.wait_ge(s["lin_ev"].sem, st.at("lin_ev", self.lin("ret_g0") + 4))

        def scores(n):
            h, jt = divmod(n, 4)
            part = slice(64 * (h % 2), 64 * (h % 2) + 64)
            if n >= 2:
                pe.wait_ge(s["st_ready"].sem, st.at("st_ready", n - 1))
            s["ret_mm"].up(nc.tensor.matmul(ps[:, 4 + n % 2, 0:T - jt * P], self.rk[part, h // 2, jt * P:(jt + 1) * P],
                                            self.rq[part, h // 2, jt * P:T], start=True, stop=True))
        scores(0)
        for n in range(16):
            h, jt = divmod(n, 4)
            if n + 1 < 16:
                scores(n + 1)
            pe.wait_ge(s["st_ready"].sem, st.at("st_ready", n + 1))
            if jt == 0 and h >= 2:
                pe.wait_ge(s["br_full"].sem, st.at("br_full", 4 + h - 1))
            mm = nc.tensor.matmul(ps[:, 6 + h % 2, jt * P:T], self.rv[:, jt, h * P:(h + 1) * P], self.st[:, n % 2, 0:T - jt * P],
                                  start=jt == 0, stop=jt == 3)
            if jt == 3:
                s["head_done"].up(mm)
            if jt == 0 and h:
                self.pe_head(pe, st, h - 1)
        self.pe_head(pe, st, 3)

    def dve_retention(self, dve, st):
        nc, s = self.nc, self.s
        dve.wait_ge(self.tables_in, self.tables_at(st, "mixer"))
        for n in range(16):
            h, jt = divmod(n, 4)
            dve.wait_ge(s["ret_mm"].sem, st.at("ret_mm", n + 1))
            s["st_ready"].up(nc.vector.scalar_tensor_tensor(self.st[:, n % 2, 0:T - jt * P], self.ps[:, 4 + n % 2, 0:T - jt * P],
                                                            E ** -0.5, self.decay[:, h, 0:T - jt * P], ALU.mult, ALU.mult))
            if h and jt:
                (self.dve_head_factor, self.dve_head_gate, lambda *a: self.dve_branch_lo(*a[:2], 4 + a[2]))[jt - 1](dve, st, h - 1)
        self.dve_head(dve, st, 3)

    def act_decays(self, act, st, tt):
        nc, s = self.nc, self.s
        act.wait_ge(s["lr_mm"].sem, st.at("lr_mm", 2))
        if tt:
            act.wait_ge(s["qk_ready"].sem, st.at("qk_ready", 2 * LEVELS))
        self.act_then(act, nc.scalar.activation(self.gf[:], self.ps[:, 4 + tt], ACT.Identity, bias=self.lr_b[:, st.index, tt:tt + 1]))
        self.act_then(act, nc.scalar.activation(self.gr[:], self.gf[:], ACT.Abs))
        self.act_then(act, nc.scalar.activation(self.gr[:], self.gr[:], ACT.Exp, scale=-1.0))
        s["la_parts"].up(nc.scalar.activation(self.gr[:], self.gr[:], ACT.Ln, bias=1.0))

    @staticmethod
    def blocks(ap, level, odd):
        return ap.rearrange("p (b o t) -> p b o t", o=2, t=1 << level)[:, :, odd]

    def dve_gla_tile(self, dve, st, tt):
        nc, s = self.nc, self.s
        v = nc.vector
        gf, gr = self.gf[:], self.gr[:]
        dve.wait_ge(s["la_parts"].sem, st.at("la_parts", tt + 1))
        self.dve_then(dve, v.scalar_tensor_tensor(gf, gf, 0.0, gr, ALU.min, ALU.subtract))
        s["la_ready"].up(v.memset(gr, 0.0))
        dve.wait_ge(s["la_ready"].sem, st.at("la_ready", tt + 1))
        self.dve_level_copy(dve, st, tt, -1)
        for l in range(LEVELS):
            n = 2 * (LEVELS * tt + l)
            dve.wait_ge(s["ex_ready"].sem, st.at("ex_ready", n + 2))
            if l < LEVELS - 1:
                if l:
                    dve.wait_ge(s["la_next"].sem, st.at("la_next", (LEVELS - 1) * tt + l))
                f_odd, f_even = (self.blocks(gf, l, o) for o in (1, 0))
                r_even = self.blocks(gr, l, 0)
                last = (1 << l) - 1
                total = f_odd[:, :, last:last + 1].to_broadcast([P, T >> (l + 1), 1 << l])
                self.dve_then(dve, v.tensor_tensor(r_even, r_even, total, ALU.add))
                total = f_even[:, :, last:last + 1].to_broadcast([P, T >> (l + 1), 1 << l])
                s["la_next"].up(v.tensor_tensor(f_odd, f_odd, total, ALU.add))
            dve.wait_ge(s["lvl_mm"].sem, st.at("lvl_mm", self.level_at(tt, max(l - 2, -1)) + 2))
            ge = self.ge[l % 2][:]
            s["qk_ready"].up(v.tensor_tensor(self.gqe[l % 2][:], self.gq[:, tt], ge, ALU.mult))
            s["qk_ready"].up(v.tensor_tensor(self.gke[l % 2][:], self.gk[:, tt], ge, ALU.mult))
            if 0 <= l - 1 < 7:
                self.dve_level_copy(dve, st, tt, l - 1)
            if tt and l == 4:
                for n in self.HEADS_BEFORE:
                    self.dve_head_factor(dve, st, n)
                    self.dve_head_gate(dve, st, n)
            if tt and l == 7:
                for n in self.HEADS_BEFORE:
                    self.dve_branch_lo(dve, st, 4 + n)

    HEADS_BEFORE = (4, 5)

    def level_at(self, tt, l):
        return 2 * (10 * tt + l + 1)

    def dve_level_copy(self, dve, st, tt, l):
        nc, s = self.nc, self.s
        mask = self.masks[:, 7 if l < 0 else l].unsqueeze(1).to_broadcast([P, TT, P])
        for hh in range(2):
            dve.wait_ge(s["lvl_mm"].sem, st.at("lvl_mm", self.level_at(tt, l) + hh + 1))
            if l < 0 and tt:
                dve.wait_ge(s["head_done"].sem, st.at("head_done", 4 + 2))
            bank = 2 * ((l + 1) % 2) + hh
            dst = self.sd[:, hh].rearrange("p (a t) -> p a t", a=TT)
            src = self.ps[:, bank].rearrange("p (a t) -> p a t", a=TT)
            s["lvl_cp"].up(nc.vector.copy_predicated(dst, mask, src))

    def act_gla_tile(self, act, st, tt):
        nc, s = self.nc, self.s
        for l in range(LEVELS):
            ge = self.ge[l % 2][:]
            if l == 0:
                act.wait_ge(s["la_ready"].sem, st.at("la_ready", tt + 1))
            else:
                act.wait_ge(s["la_next"].sem, st.at("la_next", (LEVELS - 1) * tt + l))
            n = LEVELS * tt + l
            if l >= 2:
                act.wait_ge(s["qk_ready"].sem, st.at("qk_ready", 2 * (n - 1)))
            for odd, src in ((1, self.gf[:]), (0, self.gr[:])):
                s["ex_ready"].up(nc.scalar.activation(self.blocks(ge, l, odd), self.blocks(src, l, odd), ACT.Exp, scale=1 / 16))
            if l == 8:
                self.act_across(act, st, tt, 7)
            if tt and l in (1, 3, 6):
                step = {1: self.act_head_square, 3: self.act_head_std, 6: lambda *a: self.act_branch_hi(*a[:2], 4 + a[2])}[l]
                for n in self.HEADS_BEFORE:
                    step(act, st, n)
        self.act_across(act, st, tt, 8)

    def act_across(self, act, st, tt, l):
        nc, s = self.nc, self.s
        for hh in range(2):
            act.wait_ge(s["lvl_mm"].sem, st.at("lvl_mm", self.level_at(tt, l) + hh + 1))
            if tt and l == 7:
                act.wait_ge(s["head_done"].sem, st.at("head_done", 4 + 2))
            bank = 2 * ((l + 1) % 2) + hh
            parts = [((0, P), (0, P)), ((5 * P, 6 * P), (P, 2 * P))] if l == 7 else [((P, 5 * P), (0, 4 * P))]
            for (a, b), (c, d) in parts:
                ins = nc.scalar.activation(self.so[:, hh, a:b], self.ps[:, bank, c:d], ACT.Copy)
                if (a, b) != (0, P):
                    s["so_cp"].up(ins)
                else:
                    s["act_step"].up(ins)

    def pe_gla_tile(self, pe, st, tt):
        nc, s, ps = self.nc, self.s, self.ps
        for l in range(-1, LEVELS):
            if l >= 0:
                pe.wait_ge(s["qk_ready"].sem, st.at("qk_ready", 2 * (LEVELS * tt + l) + 2))
            for hh in range(2):
                part = slice(64 * hh, 64 * hh + 64)
                q, k = (self.gq[part, tt], self.gk[part, tt]) if l < 0 else (self.gqe[l % 2][part], self.gke[l % 2][part])
                bank = 2 * ((l + 1) % 2) + hh
                if l >= 1:
                    pe.wait_ge(s["lvl_cp"].sem, st.at("lvl_cp", 16 * tt + 2 * (l - 1) + hh + 1))
                elif tt:
                    pe.wait_ge(s["so_cp"].sem, st.at("so_cp", 4))
                if l < 7:
                    todo = [(j, j, 1, j) for j in range(TT)]
                elif l == 7:
                    todo = [(0, 1, 1, 0), (2, 3, 1, 1)]
                else:
                    todo = [(0, 2, 2, 0), (1, 2, 2, 2)]
                for j, i, n, at in todo:
                    mm = nc.tensor.matmul(ps[:, bank, at * P:(at + n) * P], k[:, j * P:(j + 1) * P], q[:, i * P:(i + n) * P],
                                          start=True, stop=True)
                s["lvl_mm"].up(mm)
            if tt and l == 2:
                for n in self.HEADS_BEFORE:
                    self.pe_head(pe, st, n)
        pe.wait_ge(s["lvl_cp"].sem, st.at("lvl_cp", 16 * (tt + 1)))
        pe.wait_ge(s["so_cp"].sem, st.at("so_cp", 4 * (tt + 1)))
        for hh in range(2):
            n = 4 + 2 * tt + hh
            h = 2 * tt + hh
            pe.wait_ge(s["br_full"].sem, st.at("br_full", 4 + n - 1))
            first = True
            at = 0
            for jt in range(TT):
                v = self.gv[:, jt, h * P:(h + 1) * P]
                mm = nc.tensor.matmul(ps[:, 6 + hh, jt * P:(jt + 1) * P], v, self.sd[:, hh, jt * P:(jt + 1) * P],
                                      start=first, stop=jt == TT - 1)
                first = False
                w = (TT - 1 - jt) * P
                if w:
                    mm = nc.tensor.matmul(ps[:, 6 + hh, (jt + 1) * P:T], v, self.so[:, hh, at:at + w], start=False, stop=False)
                    at += w
            s["head_done"].up(mm)

    def pe_mixer(self, pe, st):
        nc, s, ps = self.nc, self.s, self.ps
        self.use_dsa_units()
        self.pe_squares(pe, st, 0, 5)
        self.pe_project(pe, st, "idx_q", before=self.x_tile(pe, st, KT))
        self.pe_project(pe, st, "idx_k", ("t", "turn"))
        pe.wait_ge(self.tables_in, self.tables_at(st, "mixer", later=1))
        self.pe_project(pe, st, "dsa_q0")
        self.pe_ropes(pe, st, self.ROPE_ORDER[0:3])
        self.pe_index(pe, st)
        self.pe_project(pe, st, "dsa_q1")
        self.pe_project(pe, st, "dsa_kv", ("t", (128, 128)))
        self.pe_project(pe, st, "dsa_g0")
        self.pe_project(pe, st, "dsa_g1")
        self.pe_ropes(pe, st, self.ROPE_ORDER[3:8])
        pe.wait_ge(s["kd_ready"].sem, st.at("kd_ready", 4))
        pe.wait_ge(s["lin_ev"].sem, st.at("lin_ev", self.lin("mix_dsa")))
        for i in range(DSA_UNITS + self.OUT_LAG):
            self.pe_unit_step(pe, st, i, 0, DSA_UNITS, self.dsa_unit, 1)
        pe.wait_ge(s["br_full"].sem, st.at("br_full", 1))
        self.pe_mix(pe, st, 0, "mix_dsa")
        self.pe_project(pe, st, "ret_q")
        self.pe_project(pe, st, "ret_k")
        self.pe_project(pe, st, "ret_v0", ("v", "v"))
        pe.wait_ge(s["mixed"].sem, st.at("mixed", 8))
        self.pe_ropes(pe, st, self.ROPE_ORDER[8:12])
        self.pe_project(pe, st, "ret_v1", ("v", "v"))
        self.pe_project(pe, st, "ret_g0")
        self.pe_project(pe, st, "ret_g1")
        self.pe_retention(pe, st)
        self.pe_mix(pe, st, 1, "mix_ret")
        for name in ("gla_q", "gla_k"):
            self.pe_project(pe, st, name)
        for name in ("gla_v0", "gla_v1"):
            self.pe_project(pe, st, name, ("v", "v"))
        for name in ("gla_g0", "gla_g1"):
            self.pe_project(pe, st, name)
        self.pe_project(pe, st, "gla_a", ("part", "part"))
        pe.wait_ge(s["lin_ev"].sem, st.at("lin_ev", self.lin("mix_gla")))
        pe.wait_ge(self.lr_in, 16 * (st.index_in_kind + 1))
        pe.wait_ge(s["mixed"].sem, st.at("mixed", 16))
        for tt in range(2):
            for part in range(2):
                mm = nc.tensor.matmul(ps[:, 4 + tt], self.lr_w[:, tt * P:(tt + 1) * P], self.ga[:, part], start=part == 0, stop=part == 1)
            s["lr_mm"].up(mm)
        for tt in range(2):
            self.pe_gla_tile(pe, st, tt)
        for head in (6, 7):
            self.pe_head(pe, st, head)
        self.pe_mix(pe, st, 2, "mix_gla")
        for mp in range(4):
            self.pe_project(pe, st, "out", mp=mp, at=mp, before=self.x_tile(pe, st, 2 * KT) if mp == 0 else None)
        self.pe_squares(pe, st, 1, 5)

    def act_mixer(self, act, st):
        nc, s, ps = self.nc, self.s, self.ps
        self.use_dsa_units()
        d, n = self.dram, st.index
        tables = [(self.pos[:], d["positions_2"].to_broadcast([P, T])), (self.freq[:, 0:1], d["const_freq_ret"]),
                  (self.freq[:, 1:2], d["const_freq_dsa"]), (self.swap[:, 0], d["const_swap_ret"]),
                  (self.swap[:, 1], d["const_swap_dsa"]), (self.causal[:], d["const_causal"]),
                  (self.masks[:], d["const_level_masks"].rearrange("p (l t) -> p l t", l=8))]
        x_before = lambda m: act.wait_ge(s["x_out"].sem, st.at("x_out", 0))
        act.wait_ge(s["x_ready"].sem, st.at("x_ready", 0))
        act.wait_ge(s["acts"].sem, st.at("acts", 0))
        x_before(0)
        for dst, src in tables:
            act.dma_start(dst, src).then_inc(self.tables_in, 16)
        act.dma_start(self.lr_w[:], d["gla_w_lr_2"][n]).then_inc(self.lr_in, 16)
        act.wait_ge(s["mod_ready"].sem, 2)
        self.act_squares(act, st, 0, 5, 2, lambda m: self.x[:, m], x_before)
        for m in range(KT):
            act.wait_ge(s["t_ready"].sem, st.at("t_ready", m + 1))
            h = self.mx_h[:, m]
            t = s["h_ready"].up(nc.scalar.activation(h, h, ACT.Identity, scale=self.mod[:, n, KT + m:KT + m + 1],
                                                     bias=self.mod[:, n, m:m + 1]))
            act.wait_ge(s["h_ready"].sem, t)
            s["xh_ready"].up(nc.scalar.activation(self.xh[:, m], h, ACT.Copy))
        self.act_waves(act, st, 1)
        self.act_project(act, st, "idx_q", [self.iq[:, 0], self.iq[:, 1]])
        self.act_project(act, st, "idx_k", [self.ik[:], self.iw[:]], scale=(1.0, 0.5),
                         srcs=[ps[:, 0], ps[:, 1, 0:P].rearrange("p (r w) -> p r w", r=4)[:, :, 0:4]])
        for q in range(2):
            self.act_project(act, st, f"dsa_q{q}", [self.dq[:, 2 * q], self.dq[:, 2 * q + 1]], scale=(self.Q_SCALE,) * 2)
            if q == 0:
                self.act_index(act, st)
        self.act_project(act, st, "dsa_kv", [self.dk[:], self.dv[:]], srcs=[ps[:, 0], ps[:, 1].rearrange("p (r w) -> p r w", r=4)])
        for q in range(2):
            self.act_project(act, st, f"dsa_g{q}", [self.mx_g[:, 2 * q], self.mx_g[:, 2 * q + 1]], ACT.Silu)
        for i in range(DSA_UNITS + self.OUT_LAG):
            self.act_unit_step(act, st, i, 0, DSA_UNITS, self.dsa_unit)
        for tile in range(4):
            self.act_branch_hi(act, st, tile)
        act.dma_start(self.decay[:], d["const_decay"].rearrange("p (h t) -> p h t", h=4)).then_inc(self.tables_in, 16)
        self.act_mix(act, st, 0, "mix_dsa")
        self.act_waves(act, st, 0)
        for name, buf in (("ret_q", self.rq), ("ret_k", self.rk)):
            self.act_project(act, st, name, [buf[:, 0], buf[:, 1]])
        self.act_values(act, st, "ret", self.rv)
        self.act_retention(act, st)
        self.act_mix(act, st, 1, "mix_ret")
        for name, buf, scale in (("gla_q", self.gq, E ** -0.5), ("gla_k", self.gk, 1.0)):
            self.act_project(act, st, name, [buf[:, 0], buf[:, 1]], scale=(scale, scale))
        self.act_values(act, st, "gla", self.gv)
        self.act_project(act, st, "gla_a", [self.ga[:, 0], self.ga[:, 1]], srcs=[ps[0:16, 0], ps[0:16, 1]])
        for tt in range(2):
            self.act_decays(act, st, tt)
            self.act_gla_tile(act, st, tt)
        for step in (self.act_head_square, self.act_head_rest):
            for head in (6, 7):
                step(act, st, head)
        self.act_mix(act, st, 2, "mix_gla")
        for m in range(KT):
            act.wait_ge(s["mixed"].sem, st.at("mixed", 16 + m + 1))
            s["xh_ready"].up(nc.scalar.activation(self.xh[:, m], self.mx_y[:, m], ACT.Copy))
        for mp in range(4):
            self.act_project(act, st, "out", [self.mx_h[:, 2 * mp], self.mx_h[:, 2 * mp + 1]], mp=mp, at=mp)
        self.act_squares(act, st, 1, 5, 2, lambda m: self.mx_h[:, m],
                         lambda m: act.wait_ge(s["lin_ev"].sem, st.at("lin_ev", self.lin("out") + m + 1)), ring=True)

    def act_values(self, act, st, b, buf):
        for q in range(2):
            self.act_project(act, st, f"{b}_v{q}", [buf[:, 2 * m:2 * m + 2, 256 * q:256 * q + 256] for m in range(2)],
                             srcs=[self.ps[:, m].rearrange("p (r w) -> p r w", r=2) for m in range(2)])
        for q in range(2):
            self.act_project(act, st, f"{b}_g{q}", [self.mx_g[:, 2 * q], self.mx_g[:, 2 * q + 1]], ACT.Silu)

    def act_retention(self, act, st):
        for h in range(4):
            self.act_head_square(act, st, h)
            self.act_head_rest(act, st, h)

    def dve_mixer(self, dve, st):
        nc, s, ps = self.nc, self.s, self.ps
        self.use_dsa_units()
        n = st.index
        self.dve_angles(dve, st, 1)
        self.dve_squares(dve, st, 0, False)
        for m in range(KT):
            s["t_ready"].up(nc.vector.tensor_tensor(self.mx_h[:, m], self.x[:, m], self.std[:], ALU.mult))
        for m in range(KT):
            dve.wait_ge(s["xh_ready"].sem, st.at("xh_ready", m + 1))
            s["acts"].up(nc.vector.tensor_tensor(self.xl[:, m], self.mx_h[:, m], self.xh[:, m].bitcast(F32), ALU.subtract))
        dve.wait_ge(s["waves"].sem, 2)
        self.dve_ropes(dve, st, self.ROPE_ORDER[0:3])
        s["ikd_ready"].up(nc.vector.tensor_copy(self.ik[64:128], self.ik[0:64]))
        self.dve_index(dve, st)
        for qt in (1, 2):
            for _ in range(TOPK // 8):
                self.dve_choose_round(dve, qt)
            self.dve_choose_biases(dve, qt)
        for _ in range(EARLY_ROUNDS):
            self.dve_choose_round(dve, 3)
        self.dve_ropes(dve, st, self.ROPE_ORDER[3:8])
        for kv in range(2):
            for half in range(2):
                s["kd_ready"].up(nc.vector.tensor_copy(self.kd[64 * half:64 * half + 64, kv], self.dk[64 * kv:64 * kv + 64]))
        for i in range(DSA_UNITS + self.OUT_LAG):
            self.dve_unit_step(dve, st, i, 0, DSA_UNITS, self.dsa_unit)
            if i < TOPK // 8 - EARLY_ROUNDS:
                self.dve_choose_round(dve, 3)
            if i == TOPK // 8 - EARLY_ROUNDS:
                self.dve_choose_biases(dve, 3)
        for tile in range(4):
            dve.wait_ge(s["pv_done"].sem, st.at("pv_done", DSA_UNITS - 6 + 2 * tile))
            if tile >= 2:
                dve.wait_ge(s["br_lo"].sem, st.at("br_lo", tile - 1))
            s["br_full"].up(nc.vector.tensor_tensor(self.mx_t[:, tile % 2], ps[:, self.DSA_BANKS[tile]], self.mx_g[:, tile], ALU.mult))
            self.dve_branch_lo(dve, st, tile)
        self.dve_mix(dve, st, 0, "mix_dsa")
        self.dve_angles(dve, st, 0)
        dve.wait_ge(s["waves"].sem, 4)
        self.dve_ropes(dve, st, self.ROPE_ORDER[8:12])
        self.dve_retention(dve, st)
        self.dve_mix(dve, st, 1, "mix_ret")
        for hh in range(2):
            s["sd_zero"].up(nc.vector.memset(self.sd[:, hh], 0.0))
        for tt in range(2):
            self.dve_gla_tile(dve, st, tt)
        for head in (6, 7):
            self.dve_head(dve, st, head)
        self.dve_mix(dve, st, 2, "mix_gla")
        for m in range(KT):
            dve.wait_ge(s["xh_ready"].sem, st.at("xh_ready", KT + m + 1))
            s["acts"].up(nc.vector.tensor_tensor(self.xl[:, m], self.mx_y[:, m], self.xh[:, m].bitcast(F32), ALU.subtract))
        self.dve_squares(dve, st, 1, True)
        for m in range(KT):
            t = s["t_ready"].up(nc.vector.tensor_tensor(self.mx_h[:, m], self.mx_h[:, m], self.std[:], ALU.mult))
            dve.wait_ge(s["t_ready"].sem, t)
            s["x_out"].up(nc.vector.scalar_tensor_tensor(self.x[:, m], self.mx_h[:, m], self.mod[:, n, 2 * KT + m:2 * KT + m + 1],
                                                         self.x[:, m], ALU.mult, ALU.add))

    def stage_end(self, index):
        return {}, []

    def sp_end(self, sp, st):
        sp.wait_ge(self.s["x_ready"].sem, st.at("x_ready", 0))
        dst = self.dram["out_t"].rearrange("(k p) t -> p k t", p=P)
        for m in range(0, KT, 2):
            if st.at("x_out", 0):
                sp.wait_ge(self.s["x_out"].sem, st.at("x_out", m + 2 - KT))
            sp.dma_start(dst[:, m:m + 2], self.x[:, m:m + 2]).then_inc(self.out_done, 16)
        sp.wait_ge(self.out_done, 16 * (KT // 2))

    def walk(self, eng, programs):
        for st in self.stages:
            if st.kind in programs:
                programs[st.kind](eng, st)

    def check_counts(self):
        for n, v in self.end.items():
            assert self.s[n].made == v or n in ("acc", "w_lo"), (n, self.s[n].made, v)
        assert self.s["acc"].made == PRIMED["acc"] + 2 * self.chunks

    def programs(self, block):
        @block.sync
        def _(sp):
            self.sp_weights(sp)
            self.walk(sp, dict(end=self.sp_end))

        @block.gpsimd
        def _(pool):
            self.pool_start(pool, self.stages[0])
            self.pool_weights(pool)

        @block.tensor
        def _(pe):
            self.walk(pe, dict(start=self.pe_start, ffn=self.pe_ffn, pool=self.pe_pool, attn=self.pe_attn,
                               mixer=self.pe_mixer))

        @block.scalar
        def _(act):
            self.walk(act, dict(start=self.act_start, ffn=self.act_ffn, pool=self.act_pool, attn=self.act_attn,
                               mixer=self.act_mixer))

        @block.vector
        def _(dve):
            self.walk(dve, dict(start=self.dve_start, ffn=self.dve_ffn, pool=self.dve_pool, attn=self.dve_attn,
                               mixer=self.dve_mixer))


STAGES = [("start", 0), ("ffn", 0), ("pool", 0), ("ffn", 1), ("ffn", 2), ("attn", 0), ("ffn", 3),
          ("mixer", 0), ("mixer", 1), ("end", 0)]


def build(nc, dram, stages):
    with ExitStack() as ctx:
        k = Kernel(nc, dram, stages, ctx)
        with nc.Block() as block:
            k.programs(block)
        k.check_counts()


def by_feature(a):
    a = np.asarray(a)
    return np.ascontiguousarray(a.reshape(-1, P).T)


def arrays(inputs):
    out = {n: np.ascontiguousarray(a) for n, a in inputs.items()
           if n not in ("x", "ln_gain", "ln_bias", "pool_scale", "ada_b_2", "pre_norm_2", "post_norm_2",
                        "gla_b_lr_2", "c_2")}
    out["ada_w_2"] = np.ascontiguousarray(np.asarray(inputs["ada_w_2"]).transpose(1, 0, 2)).reshape(D, -1)
    out["x_t"] = np.ascontiguousarray(np.asarray(inputs["x"])[0].T)
    out["ln"] = np.concatenate([by_feature(inputs["ln_gain"]), by_feature(inputs["ln_bias"])], axis=1)
    for n in ("pool_scale", "ada_b_2", "pre_norm_2", "post_norm_2", "gla_b_lr_2", "c_2"):
        out[n] = by_feature(inputs[n])
    for n, a in CONSTANTS.items():
        out["const_" + n] = a
    return out


def kernel(**inputs):
    import concourse.bacc as bacc
    from concourse.bass_utils import run_bass_kernel_spmd as run

    nc = bacc.Bacc("TRN2", target_bir_lowering=False, num_devices=1)
    given = {"in_" + n: a for n, a in arrays(inputs).items()}
    dram = {n[3:]: nc.dram_tensor(n, a.shape, mybir.dt.from_np(a.dtype), kind="ExternalInput").ap() for n, a in given.items()}
    dram["out_t"] = nc.dram_tensor("out_t", (D, T), F32, kind="ExternalOutput").ap()
    build(nc, dram, STAGES)
    got = run(nc, [given], core_ids=[0]).results[0]["out_t"]
    return np.ascontiguousarray(got.T).reshape(1, T, D)
```
